# Optimizing a Trainium2 kernel written in Bass

```python
import jax, jax.numpy as jnp
from jax import lax
import numpy as np

D_MODEL = 1024
BATCH = 1
SEQ = 1024
DEPTH = 1
DEC_BATCH = 8
DEC_SEQ = 8
PAST_LEN = 8192
PAGE_SIZE = 128

N_META = 16
CHUNK = 64
CONV_W = 4
GDN_HEADS = 4
GDN_DK = 128
GDN_DV = 128
SSD_HEADS = 8
SSD_P = 64
SSD_N = 128
SSD_GROUPS = 2
GDN_QK = GDN_HEADS * GDN_DK
GDN_V = GDN_HEADS * GDN_DV
SSD_INNER = SSD_HEADS * SSD_P
SSD_BC = SSD_GROUPS * SSD_N
MIX_WIDTH = GDN_V + SSD_INNER
GDN_CONV_DIM = 2 * GDN_QK + GDN_V
SSD_CONV_DIM = SSD_INNER + 2 * SSD_BC
IN_DIM = GDN_CONV_DIM + GDN_V + 2 * GDN_HEADS + SSD_INNER + SSD_CONV_DIM + SSD_HEADS
N_EGROUPS = 4
E_PER_GROUP = 8
N_EXPERTS = N_EGROUPS * E_PER_GROUP
TOP_K = 2
D_EXPERT = D_MODEL // 2
MOE_BLOCK = 128
DEEPNORM_ALPHA = (2 * DEPTH) ** 0.25
DEEPNORM_BETA = (8 * DEPTH) ** -0.25
EPS = 1e-6

kernel_name = 'hymba_gdn_ssd_hmoe_step'

def _layer_norm(x, g, b):
    xf = x.astype(jnp.float32)
    mu = jnp.mean(xf, axis=-1, keepdims=True)
    var = jnp.mean(jnp.square(xf - mu), axis=-1, keepdims=True)
    return ((xf - mu) * lax.rsqrt(var + EPS) * g.astype(jnp.float32) + b.astype(jnp.float32)).astype(x.dtype)

def _rms(x):
    return x * lax.rsqrt(jnp.mean(jnp.square(x), axis=-1, keepdims=True) + EPS)

def _l2norm(x):
    return x * lax.rsqrt(jnp.sum(jnp.square(x), axis=-1, keepdims=True) + EPS)

def _causal_conv(x, buf, w, b):
    L = x.shape[1]
    xp = jnp.concatenate([buf.astype(x.dtype), x], axis=1)
    y = sum(xp[:, i:i + L] * w[i] for i in range(CONV_W))
    if b is not None:
        y = y + b
    return jax.nn.silu(y), xp[:, L:]

def _to_chunks(a, chunk):
    b_, h_, L = a.shape[:3]
    nc = -(-L // chunk)
    a = jnp.pad(a, [(0, 0), (0, 0), (0, nc * chunk - L)] + [(0, 0)] * (a.ndim - 3))
    a = a.reshape((b_, h_, nc, chunk) + a.shape[3:])
    return jnp.moveaxis(a, 2, 0)

def _from_chunks(a, L):
    a = jnp.moveaxis(a, 0, 2)
    a = a.reshape(a.shape[:2] + (-1,) + a.shape[4:])
    return a[:, :, :L]

def _decay_matrices(g):
    gam = jnp.cumsum(g, axis=-1)
    c = g.shape[-1]
    causal = jnp.tril(jnp.ones((c, c), dtype=bool))
    diff = gam[..., :, None] - gam[..., None, :]
    return gam, jnp.exp(jnp.where(causal, diff, -jnp.inf))

def _gdn_segment(q, k, v, g, beta, s0, chunk):
    L = q.shape[2]
    qc, kc, vc, gc, bc = [_to_chunks(a, chunk) for a in (q, k, v, g, beta)]
    gam, dec = _decay_matrices(gc)
    eye = jnp.eye(chunk, dtype=qc.dtype)
    kk = jnp.einsum('nbhcd,nbhed->nbhce', kc, kc)
    m = eye + bc[..., :, None] * kk * dec * (1.0 - eye)
    u_t = lax.linalg.triangular_solve(m, bc[..., None] * vc, left_side=True, lower=True)
    w = lax.linalg.triangular_solve(m, (bc * jnp.exp(gam))[..., None] * kc, left_side=True, lower=True)
    qk = jnp.einsum('nbhcd,nbhed->nbhce', qc, kc) * dec
    q_dec = qc * jnp.exp(gam)[..., None]
    k_dec = kc * jnp.exp(gam[..., -1:] - gam)[..., None]
    g_end = jnp.exp(gam[..., -1])

    def step(s, inp):
        u_c, w_c, qk_c, q_c, k_c, ge = inp
        u = u_c - jnp.einsum('bhcd,bhde->bhce', w_c, s)
        o = jnp.einsum('bhcd,bhde->bhce', q_c, s) + jnp.einsum('bhce,bhef->bhcf', qk_c, u)
        s = ge[..., None, None] * s + jnp.einsum('bhcd,bhce->bhde', k_c, u)
        return s, o

    s, o = lax.scan(step, s0, (u_t, w, qk, q_dec, k_dec, g_end))
    return _from_chunks(o, L), s

def _ssd_segment(x, dt, g, bm, cm, h0, chunk):
    L = x.shape[2]
    xc, dtc, gc, bc, cc = [_to_chunks(a, chunk) for a in (x, dt, g, bm, cm)]
    gam, dec = _decay_matrices(gc)
    xdt = xc * dtc[..., None]
    cb = jnp.einsum('nbhts,nbhjs->nbhtj', cc, bc) * dec
    c_dec = cc * jnp.exp(gam)[..., None]
    b_dec = bc * jnp.exp(gam[..., -1:] - gam)[..., None]
    g_end = jnp.exp(gam[..., -1])

    def step(hs, inp):
        xdt_c, cb_c, c_c, b_c, ge = inp
        y = jnp.einsum('bhts,bhps->bhtp', c_c, hs) + jnp.einsum('bhtj,bhjp->bhtp', cb_c, xdt_c)
        hs = ge[..., None, None] * hs + jnp.einsum('bhjp,bhjs->bhps', xdt_c, b_c)
        return hs, y

    hs, y = lax.scan(step, h0, (xdt, cb, c_dec, b_dec, g_end))
    return _from_chunks(y, L), hs

def _run_segments(segment_fn, seqs, state, segments):
    outs, start = [], 0
    for length, chunk in segments:
        part = [s[:, :, start:start + length] for s in seqs]
        out, state = segment_fn(*part, state, chunk)
        outs.append(out)
        start += length
    return jnp.concatenate(outs, axis=2), state

def _mixer(h, s_a, conv_a, s_b, conv_b, segments, w_in, gdn_conv_w, gdn_a_log, gdn_dt_bias, gdn_norm_w,
           ssd_conv_w, ssd_conv_b, ssd_a_log, ssd_dt_bias, ssd_d, ssd_norm_w, w_out):
    f32 = jnp.float32
    bsz, L, _ = h.shape
    proj = h @ w_in
    cuts = np.cumsum([GDN_CONV_DIM, GDN_V, GDN_HEADS, GDN_HEADS, SSD_INNER, SSD_CONV_DIM]).tolist()
    qkv, z_a, b_a, a_a, z_b, xbc, dt_b = jnp.split(proj, cuts, axis=-1)

    def heads(t, d):
        return t.reshape(bsz, L, -1, d).transpose(0, 2, 1, 3)

    qkv, new_conv_a = _causal_conv(qkv, conv_a, gdn_conv_w, None)
    q, k, v = jnp.split(qkv.astype(f32), [GDN_QK, 2 * GDN_QK], axis=-1)
    q = _l2norm(heads(q, GDN_DK)) * (GDN_DK ** -0.5)
    k = _l2norm(heads(k, GDN_DK))
    v = heads(v, GDN_DV)
    beta = jax.nn.sigmoid(b_a.astype(f32)).transpose(0, 2, 1)
    g_a = (-jnp.exp(gdn_a_log.astype(f32))[:, None]
           * jax.nn.softplus(a_a.astype(f32) + gdn_dt_bias.astype(f32)).transpose(0, 2, 1))
    o_a, s_a = _run_segments(_gdn_segment, (q, k, v, g_a, beta), s_a.astype(f32), segments)
    o_a = o_a.transpose(0, 2, 1, 3)
    o_a = _rms(o_a) * gdn_norm_w.astype(f32) * jax.nn.silu(z_a.astype(f32)).reshape(bsz, L, GDN_HEADS, GDN_DV)
    o_a = o_a.reshape(bsz, L, GDN_V)

    xbc, new_conv_b = _causal_conv(xbc, conv_b, ssd_conv_w, ssd_conv_b)
    xs, bm, cm = jnp.split(xbc.astype(f32), [SSD_INNER, SSD_INNER + SSD_BC], axis=-1)
    xs = heads(xs, SSD_P)
    rep = SSD_HEADS // SSD_GROUPS
    bm = jnp.repeat(heads(bm, SSD_N), rep, axis=1)
    cm = jnp.repeat(heads(cm, SSD_N), rep, axis=1)
    dt = jax.nn.softplus(dt_b.astype(f32) + ssd_dt_bias.astype(f32)).transpose(0, 2, 1)
    g_b = -jnp.exp(ssd_a_log.astype(f32))[:, None] * dt
    y_b, s_b = _run_segments(_ssd_segment, (xs, dt, g_b, bm, cm), s_b.astype(f32), segments)
    y_b = y_b + ssd_d.astype(f32)[:, None, None] * xs
    y_b = y_b.transpose(0, 2, 1, 3).reshape(bsz, L, SSD_INNER) * jax.nn.silu(z_b.astype(f32))
    y_b = _rms(y_b.reshape(bsz, L, SSD_GROUPS, -1)).reshape(bsz, L, SSD_INNER) * ssd_norm_w.astype(f32)

    mix = jnp.concatenate([o_a, y_b], axis=-1).astype(h.dtype) @ w_out
    return mix.astype(h.dtype), s_a, new_conv_a, s_b, new_conv_b

def _moe(h, router_g, router_e, w1, w3, w2):
    T = h.shape[0]
    hf = h.astype(jnp.float32)
    g_prob = jax.nn.softmax(hf @ router_g.astype(jnp.float32), axis=-1)
    g_val, g_idx = lax.top_k(g_prob, 1)
    e_logits = (hf @ router_e.astype(jnp.float32)).reshape(T, N_EGROUPS, E_PER_GROUP)
    e_logits = jnp.take_along_axis(e_logits, g_idx[:, :, None], axis=1)[:, 0]
    e_val, e_idx = lax.top_k(jax.nn.softmax(e_logits, axis=-1), TOP_K)
    gate = g_val * e_val / jnp.sum(e_val, axis=-1, keepdims=True)
    expert = g_idx * E_PER_GROUP + e_idx

    A = T * TOP_K
    e_flat = expert.reshape(-1)
    tok_flat = jnp.repeat(jnp.arange(T, dtype=jnp.int32), TOP_K)
    w_flat = gate.reshape(-1)
    order = jnp.argsort(e_flat)
    e_sorted = e_flat[order]
    counts = jnp.bincount(e_flat, length=N_EXPERTS)
    padded = ((counts + MOE_BLOCK - 1) // MOE_BLOCK) * MOE_BLOCK
    pad_end = jnp.cumsum(padded)
    pad_start = pad_end - padded
    start = jnp.cumsum(counts) - counts
    dest = pad_start[e_sorted] + (jnp.arange(A) - start[e_sorted])
    nb = -(-A // MOE_BLOCK) + N_EXPERTS
    slot_tok = jnp.zeros((nb * MOE_BLOCK,), jnp.int32).at[dest].set(tok_flat[order])
    slot_w = jnp.zeros((nb * MOE_BLOCK,), jnp.float32).at[dest].set(w_flat[order])
    block_exp = jnp.minimum(jnp.searchsorted(pad_end, jnp.arange(nb) * MOE_BLOCK, side='right'), N_EXPERTS - 1)

    def block(args):
        tok, e = args
        xb = h[tok]
        return (jax.nn.silu(xb @ w1[e]) * (xb @ w3[e])) @ w2[e]

    out = lax.map(block, (slot_tok.reshape(nb, MOE_BLOCK), block_exp))
    y = jnp.zeros((T, D_MODEL), jnp.float32).at[slot_tok].add(
        out.reshape(-1, D_MODEL).astype(jnp.float32) * slot_w[:, None])
    return y.astype(h.dtype)

def _trunk(x, s_a, conv_a, s_b, conv_b, segments, params):
    (w_in, gdn_conv_w, gdn_a_log, gdn_dt_bias, gdn_norm_w, ssd_conv_w, ssd_conv_b, ssd_a_log,
     ssd_dt_bias, ssd_d, ssd_norm_w, w_out, ln1_g, ln1_b, router_g, router_e, w1, w3, w2, ln2_g, ln2_b) = params
    bsz, L, _ = x.shape
    out_sa, out_ca, out_sb, out_cb = [], [], [], []
    for l in range(DEPTH):
        mix, sa, ca, sb, cb = _mixer(x, s_a[l], conv_a[l], s_b[l], conv_b[l], segments, w_in[l], gdn_conv_w[l],
                                     gdn_a_log[l], gdn_dt_bias[l], gdn_norm_w[l], ssd_conv_w[l], ssd_conv_b[l],
                                     ssd_a_log[l], ssd_dt_bias[l], ssd_d[l], ssd_norm_w[l], w_out[l])
        out_sa.append(sa.astype(s_a.dtype))
        out_ca.append(ca.astype(conv_a.dtype))
        out_sb.append(sb.astype(s_b.dtype))
        out_cb.append(cb.astype(conv_b.dtype))
        x = _layer_norm(DEEPNORM_ALPHA * x + mix, ln1_g[l], ln1_b[l])
        ffn = _moe(x.reshape(bsz * L, D_MODEL), router_g[l], router_e[l], w1[l], w3[l], w2[l]).reshape(x.shape)
        x = _layer_norm(DEEPNORM_ALPHA * x + ffn, ln2_g[l], ln2_b[l])
    return (x, jnp.stack(out_sa), jnp.stack(out_ca), jnp.stack(out_sb), jnp.stack(out_cb))

def setup_inputs(seed: int = 0) -> dict:
    key = jax.random.key(seed)
    ks = jax.random.split(key, 32)
    f32 = jnp.float32
    nrm = lambda k, shape, scale: jax.random.normal(k, shape, f32) * scale

    def dt_bias(k, shape):
        dt = jnp.exp(jax.random.uniform(k, shape, f32, np.log(1e-3), np.log(1e-1)))
        return dt + jnp.log(-jnp.expm1(-dt))

    return {
        'x_prompt': nrm(ks[0], (BATCH, SEQ, D_MODEL), 1.0),
        'x_sample': nrm(ks[1], (DEC_BATCH, DEC_SEQ, D_MODEL), 1.0),
        'state_gdn': nrm(ks[2], (DEPTH, DEC_BATCH, GDN_HEADS, GDN_DK, GDN_DV), 0.1),
        'state_gdn_conv': nrm(ks[3], (DEPTH, DEC_BATCH, CONV_W - 1, GDN_CONV_DIM), 1.0),
        'state_ssd': nrm(ks[4], (DEPTH, DEC_BATCH, SSD_HEADS, SSD_P, SSD_N), 0.1),
        'state_ssd_conv': nrm(ks[5], (DEPTH, DEC_BATCH, CONV_W - 1, SSD_CONV_DIM), 1.0),
        'meta_tokens': nrm(ks[6], (N_META, D_MODEL), 1.0),
        'w_in': nrm(ks[7], (DEPTH, D_MODEL, IN_DIM), D_MODEL ** -0.5),
        'gdn_conv_w': nrm(ks[8], (DEPTH, CONV_W, GDN_CONV_DIM), CONV_W ** -0.5),
        'gdn_a_log': jnp.log(jax.random.uniform(ks[9], (DEPTH, GDN_HEADS), f32, 1.0, 16.0)),
        'gdn_dt_bias': dt_bias(ks[10], (DEPTH, GDN_HEADS)),
        'gdn_norm_w': 1.0 + nrm(ks[11], (DEPTH, GDN_DV), 0.05),
        'ssd_conv_w': nrm(ks[12], (DEPTH, CONV_W, SSD_CONV_DIM), CONV_W ** -0.5),
        'ssd_conv_b': nrm(ks[13], (DEPTH, SSD_CONV_DIM), 0.02),
        'ssd_a_log': jnp.log(jax.random.uniform(ks[14], (DEPTH, SSD_HEADS), f32, 1.0, 16.0)),
        'ssd_dt_bias': dt_bias(ks[15], (DEPTH, SSD_HEADS)),
        'ssd_d': 1.0 + nrm(ks[16], (DEPTH, SSD_HEADS), 0.05),
        'ssd_norm_w': 1.0 + nrm(ks[17], (DEPTH, SSD_INNER), 0.05),
        'w_out': nrm(ks[18], (DEPTH, MIX_WIDTH, D_MODEL), MIX_WIDTH ** -0.5 * DEEPNORM_BETA),
        'ln1_g': 1.0 + nrm(ks[19], (DEPTH, D_MODEL), 0.05),
        'ln1_b': nrm(ks[20], (DEPTH, D_MODEL), 0.02),
        'router_g': nrm(ks[21], (DEPTH, D_MODEL, N_EGROUPS), D_MODEL ** -0.5),
        'router_e': nrm(ks[22], (DEPTH, D_MODEL, N_EXPERTS), D_MODEL ** -0.5),
        'w1': nrm(ks[23], (DEPTH, N_EXPERTS, D_MODEL, D_EXPERT), D_MODEL ** -0.5),
        'w3': nrm(ks[24], (DEPTH, N_EXPERTS, D_MODEL, D_EXPERT), D_MODEL ** -0.5),
        'w2': nrm(ks[25], (DEPTH, N_EXPERTS, D_EXPERT, D_MODEL), D_EXPERT ** -0.5 * DEEPNORM_BETA),
        'ln2_g': 1.0 + nrm(ks[26], (DEPTH, D_MODEL), 0.05),
        'ln2_b': nrm(ks[27], (DEPTH, D_MODEL), 0.02),
    }

def reference(x_prompt, x_sample, state_gdn, state_gdn_conv, state_ssd, state_ssd_conv, meta_tokens,
              w_in, gdn_conv_w, gdn_a_log, gdn_dt_bias, gdn_norm_w, ssd_conv_w, ssd_conv_b, ssd_a_log,
              ssd_dt_bias, ssd_d, ssd_norm_w, w_out, ln1_g, ln1_b, router_g, router_e, w1, w3, w2, ln2_g, ln2_b):
    params = (w_in, gdn_conv_w, gdn_a_log, gdn_dt_bias, gdn_norm_w, ssd_conv_w, ssd_conv_b, ssd_a_log,
              ssd_dt_bias, ssd_d, ssd_norm_w, w_out, ln1_g, ln1_b, router_g, router_e, w1, w3, w2, ln2_g, ln2_b)

    bp, sp = x_prompt.shape[0], x_prompt.shape[1]
    meta = jnp.broadcast_to(meta_tokens.astype(x_prompt.dtype), (bp, N_META, D_MODEL))
    xp = jnp.concatenate([meta, x_prompt], axis=1)
    zs_a = jnp.zeros((DEPTH, bp, GDN_HEADS, GDN_DK, GDN_DV), state_gdn.dtype)
    zc_a = jnp.zeros((DEPTH, bp, CONV_W - 1, GDN_CONV_DIM), state_gdn_conv.dtype)
    zs_b = jnp.zeros((DEPTH, bp, SSD_HEADS, SSD_P, SSD_N), state_ssd.dtype)
    zc_b = jnp.zeros((DEPTH, bp, CONV_W - 1, SSD_CONV_DIM), state_ssd_conv.dtype)
    yp, p_sa, p_ca, p_sb, p_cb = _trunk(xp, zs_a, zc_a, zs_b, zc_b, [(N_META, N_META), (sp, CHUNK)], params)
    y_prompt = yp[:, N_META:]

    ls = x_sample.shape[1]
    y_sample, s_sa, s_ca, s_sb, s_cb = _trunk(x_sample, state_gdn, state_gdn_conv, state_ssd, state_ssd_conv,
                                              [(ls, min(CHUNK, ls))], params)
    return (y_prompt, y_sample, p_sa, p_ca, p_sb, p_cb, s_sa, s_ca, s_sb, s_cb)


_drawn_inputs = setup_inputs


def setup_inputs(seed=0):
    import zlib

    import numpy as np

    out = dict(_drawn_inputs(seed))
    spreads = {}
    factors = {'gdn_norm_w': 3.638, 'ssd_d': 3.714, 'ssd_norm_w': 3.047, 'ln2_b': 3.12}
    for name, (base, spread) in spreads.items():
        noise = np.random.default_rng([zlib.crc32(name.encode()), seed]).standard_normal(out[name].shape)
        drawn = base * np.exp(spread * noise) if base else spread * noise
        out[name] = __import__('jax').numpy.asarray(drawn.astype(out[name].dtype))
    for name, factor in factors.items():
        out[name] = (out[name] * factor).astype(out[name].dtype)
    return out
```

```python
from contextlib import ExitStack

import numpy as np

import concourse.bass as bass
from concourse import mybir

F32 = mybir.dt.float32
I32 = mybir.dt.int32
ALU = mybir.AluOpType
ACT = mybir.ActivationFunctionType
AX = mybir.AxisListType.X

P = 128
D = 1024
KT = D // P
META, SEQ = 16, 1024
SB, SL = 8, 8
TP = META + SEQ
TS = SB * SL
T = TP + TS
C = 104
NT = TP // C
NTT = NT + 1
GH, DK = 4, 128
SH, SP_, SN, SG = 8, 64, 128, 2
NH = GH + SH
CT = 20
CW = 4
E, EG, EPG = 32, 4, 8
DE = 512
BLK = 128
NBMAX = (2 * T) // BLK + E
ALPHA = 2.0 ** 0.25
EPS = 1e-6
NS = 3
TN = T // NS
LEVELS = 7
SLEVELS = 3

BETA, EGAM, EREV, NBEG, DT, DTE = 0, 4, 16, 28, 32, 40
NCF = 48

START = dict.fromkeys((
    "at", "c_g", "c_sum", "cbd", "d_ps", "e_eo", "e_h3", "e_hT", "e_hT_ps", "e_hm", "e_out", "e_s", "e_xT",
    "e_xT_ps", "gm", "h_ps", "hdec", "hnew", "kd", "kgn", "kkqk_ps", "mixb", "mt_ps", "o2", "p_mm", "p_raw",
    "qkm", "qs_ps", "rlog", "snew", "x1t_ps", "xdte", "xg", "y1", "y4", "ys_ps", "z_ps"), 1)
START.update({"c_out": 16, "e_st": 16, "p_state": 32, "p_store": 32, "x1_st": 16})


def masks(n, block):
    k, m = np.arange(n)[:, None], np.arange(n)[None, :]
    same = k // block == m // block
    out = [same & (k <= m), same & (k > m)]
    for level in range(LEVELS):
        b = 2 ** level
        out.append(same & (k // (2 * b) == m // (2 * b)) & (k // b % 2 == 0) & (m // b % 2 == 1))
    return np.stack(out, 1).astype(np.float32)


def constants():
    c = {}
    c["c_masks"] = masks(C, C)
    c["c_smasks"] = masks(TS, SL)
    c["c_ident"] = np.eye(P, dtype=np.float32)
    seq = np.arange(TS) // SL
    c["c_seqrow"] = np.broadcast_to((seq[None, None, :] == np.arange(SB)[None, :, None]), (P, SB, TS)).astype(np.float32)
    c["c_seqcol"] = (seq[:, None] == np.arange(SB)[None, :]).astype(np.float32)
    valid = np.ones((C, NTT), np.float32)
    valid[TS:, NT] = 0
    c["c_valid"] = valid
    c["c_tok"] = ((np.arange(C)[:, None] + C * np.arange(NTT)[None, :]) * valid).astype(np.float32)
    c["c_iota"] = np.broadcast_to(np.arange(P, dtype=np.float32), (P, P)).copy()
    c["c_desc"] = np.broadcast_to(EPG - np.arange(EPG, dtype=np.float32), (C, EPG)).copy()
    k, m = np.arange(C)[:, None], np.arange(C)[None, :]
    c["c_before"] = (k < m).astype(np.float32)
    return c


def program(nc, a):
    ctx = ExitStack()
    with ctx:
        sem_names = {}

        starts = {}

        def sem(*names):
            for n in names:
                sem_names[n] = nc.alloc_semaphore(name=n)
                starts[n] = START.get(n.rstrip("01"), START.get(n, 0))

        def next_stage():
            nc.clear_and_free_semaphores(list(sem_names.values()))
            nc.all_engine_barrier()
            sem_names.clear()

        def begin():
            for n, s_ in sem_names.items():
                if starts[n]:
                    nc.sync.sem_inc(s_, starts[n])
            nc.all_engine_barrier()

        S = sem_names

        def sb(name, shape, dt=F32):
            return ctx.enter_context(nc.sbuf_tensor("sb_" + name, shape, dt))

        mask = sb("mask", [C, 2 + LEVELS, C])
        smask = sb("smask", [TS, 2 + LEVELS, TS])
        ident = sb("ident", [P, P])
        ones = sb("ones", [P, P])
        mhalf = sb("mhalf", [P, 32])
        seqrow = sb("seqrow", [P, SB, TS])
        seqcol = sb("seqcol", [TS, SB])
        coef = sb("coef", [C, NTT, NCF])
        gdec = sb("gdec", [C, NTT, NH])
        gend = sb("gend", [P, NT, NH])
        sgend = sb("sgend", [P, SB, NH])
        rlog = sb("rlog", [C, NTT, EG + E])
        lnrow = sb("lnrow", [P, 2, D])
        INC, GT, LV = 0, 1, 2

        arena_bytes = 182 * 1024
        arena = sb("arena", [P, arena_bytes // 4])

        class Arena:
            def __init__(self, start=0):
                self.at = start

            def __call__(self, parts, *shape):
                n = int(np.prod(shape))
                flat = arena[0:parts, self.at:self.at + n]
                self.at += n
                assert self.at <= arena_bytes // 4, (self.at * 4, shape)
                if len(shape) == 1:
                    return flat
                names = "abcd"[:len(shape)]
                return flat.rearrange(f"p ({' '.join(names)}) -> p {' '.join(names)}",
                                      **{n_: s_ for n_, s_ in zip(names, shape)})

        bank = [ctx.enter_context(nc.psum_tensor(f"bank{i}", [P, 512], F32)) for i in range(8)]
        PE, DVE = nc.tensor, nc.vector

        def bc(ap, *shape):
            return ap.unsqueeze(len(shape) - 1).broadcast_to(list(shape))

        def bc1(ap, *shape):
            return ap.unsqueeze(1).broadcast_to(list(shape))

        A = Arena()
        xT = A(P, KT, T)
        NW = 2
        wring = [A(P, KT, P) for _ in range(NW)]
        PADT = CW - 1 + TP
        SW = CW - 1 + SL
        raw = [A(P, PADT + SB * SW) for _ in range(NW)]
        acc = [A(P, T) for _ in range(NW)]
        eneg = [A(P, T) for _ in range(NW)]
        convw = A(P, CT, CW)
        convb = A(P, CT)
        past = A(P, CT, SB, CW - 1)
        wsm = A(P, KT, 16)
        hbias = A(P, NH)
        halog = A(P, NH)
        sm = A(C, NTT, 16)
        sp = [A(C, NTT, NH) for _ in range(5)]
        sgm = A(TS, SB, NH)

        sem("p_const", "p_x", "p_tap", "p_ones", "h_mm", "h_cp", "h_v", "h_a", "h_gam")
        for r in range(NW):
            sem(*[f"{n}{r}" for n in ("p_w", "p_mm", "p_raw", "p_conv", "p_exp", "p_one", "p_rec", "p_silu", "p_store", "p_state", "p_past")])

        def prompt_part(t):
            return t[:, CW - 1:PADT]

        def sample_part(t, off, n):
            return t[:, PADT:].rearrange("p (b s) -> p b s", b=SB)[:, :, off:off + n]

        begin()
        with nc.Block() as block:
            @block.sync
            def _(sp_):
                sp_.dma_start(wsm, a["w_small"]).then_inc(S["p_const"], 16)
                sp_.dma_start(hbias, a["head_bias"]).then_inc(S["p_const"], 16)
                sp_.dma_start(halog, a["head_alog"]).then_inc(S["p_const"], 16)
                sp_.dma_start(convw, a["conv_w"]).then_inc(S["p_const"], 16)
                sp_.dma_start(convb, a["conv_b"]).then_inc(S["p_const"], 16)
                sp_.dma_start(past, a["conv_past"]).then_inc(S["p_const"], 16)
                sp_.dma_start(mask[:], a["c_masks"]).then_inc(S["p_const"], 16)
                sp_.dma_start(smask[:], a["c_smasks"]).then_inc(S["p_const"], 16)
                sp_.dma_start(ident[:], a["c_ident"]).then_inc(S["p_const"], 16)
                sp_.dma_start(seqrow[:], a["c_seqrow"]).then_inc(S["p_const"], 16)
                sp_.dma_start(seqcol[:], a["c_seqcol"]).then_inc(S["p_const"], 16)
                sp_.dma_start(lnrow[:], a["ln_rows"][:, 0:2, :]).then_inc(S["p_const"], 16)

                def load(j, r):
                    sp_.wait_ge(S[f"p_mm{r}"], j + 1)
                    sp_.dma_start(wring[r], a["w_conv"][bass.ds(NW * j + r, 1)].rearrange("c p k m -> (c p) k m")).then_inc(S[f"p_w{r}"], 16)

                def store(j, r):
                    n = NW * j + r
                    sp_.wait_ge(S[f"p_raw{r}"], j + 2)
                    sp_.dma_start(a["o_pconv"][:, bass.ds(n, 1), :].rearrange("p c s -> p (c s)"), raw[r][:, TP:PADT]).then_inc(S[f"p_state{r}"], 16)
                    sp_.dma_start(a["o_sconv"][:, bass.ds(n, 1), :, :].rearrange("p c b s -> p (c b) s"), sample_part(raw[r], SL, CW - 1)).then_inc(S[f"p_state{r}"], 16)
                    sp_.wait_ge(S[f"p_silu{r}"], j + 1)
                    sp_.dma_start(a["d_conv"][:, :, bass.ds(n, 1), :].rearrange("t p c n -> p (t c) n"),
                                  acc[r][:, 0:TP].rearrange("p (t n) -> p t n", n=C)).then_inc(S[f"p_store{r}"], 16)
                    sp_.dma_start(a["d_sconv"][:, bass.ds(n, 1), :].rearrange("p c n -> p (c n)"), acc[r][:, TP:T]).then_inc(S[f"p_store{r}"], 16)

                for r in range(NW):
                    load(0, r)
                with sp_.Fori(1, CT // NW) as j:
                    before_j = sp_.snap(j - 1)
                    for r in range(NW):
                        load(j, r)
                        store(before_j, r)
                for r in range(NW):
                    store(CT // NW - 1, r)
                for r in range(NW):
                    sp_.wait_ge(S[f"p_store{r}"], 32 * (CT // NW) + 32)
                    sp_.wait_ge(S[f"p_state{r}"], 32 * (CT // NW) + 32)

            @block.scalar
            def _(act):
                for k in range(KT):
                    act.dma_start(xT[:, k, :], a["xT"][:, k, :]).then_inc(S["p_x"], 16)
                act.wait_ge(S["h_mm"], 1)
                act.activation(sm[:], bank[7][0:C, 0:NTT * 16].rearrange("p (t c) -> p t c", c=16), ACT.Copy).then_inc(S["h_cp"], 1)
                act.wait_ge(S["h_v"], 2)
                act.activation(sp[1], sp[1], ACT.Exp, scale=-1.0).then_inc(S["h_a"], 1)
                act.activation(coef[:, :, BETA:BETA + GH], sm[:, :, 0:GH], ACT.Exp, scale=-1.0).then_inc(S["h_a"], 1)
                act.activation(sp[3], halog.unsqueeze(1).broadcast_to([P, NTT, NH])[0:C], ACT.Exp).then_inc(S["h_a"], 1)
                act.wait_ge(S["h_v"], 3)
                act.activation(sp[2], sp[4], ACT.Ln).then_inc(S["h_a"], 1)
                act.wait_ge(S["h_gam"], 1)
                act.activation(coef[:, 0:NT, EGAM:EGAM + NH], bank[0][0:C, 0:NT * NH].rearrange("p (t c) -> p t c", c=NH), ACT.Exp).then_inc(S["h_a"], 1)
                act.activation(coef[:, 0:NT, EREV:EREV + NH], bank[1][0:C, 0:NT * NH].rearrange("p (t c) -> p t c", c=NH), ACT.Exp).then_inc(S["h_a"], 1)
                act.activation(gend[:], bank[2][:, 0:NT * NH].rearrange("p (t c) -> p t c", c=NH), ACT.Exp).then_inc(S["h_a"], 1)
                act.activation(coef[0:TS, NT, EGAM:EGAM + NH], bank[3][0:TS, 0:NH], ACT.Exp).then_inc(S["h_a"], 1)
                act.activation(coef[0:TS, NT, EREV:EREV + NH], bank[4][0:TS, 0:NH], ACT.Exp).then_inc(S["h_a"], 1)
                act.activation(sgend[:], bank[5][:, 0:SB * NH].rearrange("p (t c) -> p t c", c=NH), ACT.Exp).then_inc(S["h_a"], 1)
                with act.Fori(0, CT // NW) as j:
                    for r in range(NW):
                        act.wait_ge(S[f"p_mm{r}"], j + 2)
                        act.wait_ge(S[f"p_past{r}"], j + 1)
                        b0 = 3 * r
                        done = CW - 1
                        act.activation(raw[r][:, done:done + TN], bank[b0][:, 0:TN], ACT.Copy)
                        act.activation(raw[r][:, done + TN:done + 2 * TN], bank[b0 + 1][:, 0:TN], ACT.Copy)
                        act.activation(raw[r][:, done + 2 * TN:PADT], bank[b0 + 2][:, 0:TP - 2 * TN], ACT.Copy)
                        act.activation(sample_part(raw[r], CW - 1, SL), bank[b0 + 2][:, TP - 2 * TN:TN].rearrange("p (b s) -> p b s", b=SB), ACT.Copy).then_inc(S[f"p_raw{r}"], 1)
                        act.wait_ge(S[f"p_conv{r}"], j + 1)
                        act.activation(eneg[r], acc[r], ACT.Exp, scale=-1.0).then_inc(S[f"p_exp{r}"], 1)

            @block.tensor
            def _(pe):
                pe.wait_ge(S["p_const"], 16 * 12)
                pe.wait_ge(S["p_x"], 16 * KT)
                pe.wait_ge(S["p_ones"], 2)
                for t in range(NTT):
                    n = C if t < NT else TS
                    for k in range(KT):
                        last = pe.matmul(bank[7][0:n, 16 * t:16 * t + 16], xT[:, k, C * t:C * t + n], wsm[:, k, :],
                                         start=(k == 0), stop=(k == KT - 1))
                last.then_inc(S["h_mm"], 1)
                pe.wait_ge(S["h_v"], 6)
                g10 = gdec[:, 0:NT, :].rearrange("p t c -> p (t c)")
                pe.matmul(bank[0][0:C, 0:NT * NH], mask[:, INC, :], g10, start=True, stop=True)
                pe.matmul(bank[1][0:C, 0:NT * NH], mask[:, GT, :], g10, start=True, stop=True)
                pe.matmul(bank[2][:, 0:NT * NH], ones[0:C, :], g10, start=True, stop=True)
                pe.matmul(bank[3][0:TS, 0:NH], smask[:, INC, :], gdec[0:TS, NT, :], start=True, stop=True)
                pe.matmul(bank[4][0:TS, 0:NH], smask[:, GT, :], gdec[0:TS, NT, :], start=True, stop=True)
                pe.matmul(bank[5][:, 0:SB * NH], ones[0:TS, :], sgm.rearrange("p b c -> p (b c)"), start=True, stop=True).then_inc(S["h_gam"], 1)
                pe.wait_ge(S["h_a"], 10)
                with pe.Fori(0, CT // NW) as j:
                    for r in range(NW):
                        pe.wait_ge(S[f"p_w{r}"], 16 * j + 16)
                        pe.wait_ge(S[f"p_raw{r}"], j + 1)
                        for s in range(NS):
                            for k in range(KT):
                                last = pe.matmul(bank[3 * r + s][:, 0:TN], wring[r][:, k, :], xT[:, k, TN * s:TN * s + TN],
                                                 start=(k == 0), stop=(k == KT - 1))
                        last.then_inc(S[f"p_mm{r}"], 1)

            @block.vector
            def _(dve):
                dve.memset(ones[:], 1.0).then_inc(S["p_ones"], 1)
                dve.memset(mhalf[:], -0.5)
                dve.memset(coef[:], 0.0)
                dve.memset(gdec[:], 0.0)
                dve.memset(rlog[:], 0.0)
                dve.memset(raw[0][:, 0:CW - 1], 0.0)
                dve.memset(raw[1][:, 0:CW - 1], 0.0)
                dve.memset(bank[7][:], 0.0).then_inc(S["p_ones"], 1)
                dve.wait_ge(S["p_const"], 16 * 12)
                dve.wait_ge(S["h_cp"], 1)
                dve.tensor_tensor(sp[0], sm[:, :, 4:16], bc1(hbias[0:C], C, NTT, NH), ALU.add).then_inc(S["h_v"], 1)
                dve.wait_ge(S["h_v"], 1)
                dve.scalar_tensor_tensor(sp[1], sp[0], -1.0, sp[0], ALU.mult, ALU.max).then_inc(S["h_v"], 1)
                dve.wait_ge(S["h_a"], 3)
                dve.tensor_scalar(sp[4], sp[1], 1.0, None, ALU.add).then_inc(S["h_v"], 1)
                dve.wait_ge(S["h_a"], 4)
                d = gdec
                dve.tensor_scalar(d[:], sp[4], 1.0, 1e-30, ALU.subtract, ALU.max).then_inc(S["h_v"], 1)
                dve.wait_ge(S["h_v"], 4)
                dve.reciprocal(d[:], d[:]).then_inc(S["p_tap"], 1)
                dve.wait_ge(S["p_tap"], 1)
                dve.tensor_tensor(sp[2], sp[2], d[:], ALU.mult).then_inc(S["p_tap"], 1)
                dve.tensor_scalar(sp[4], sp[4], 1.0, None, ALU.is_equal).then_inc(S["p_tap"], 1)
                dve.wait_ge(S["p_tap"], 3)
                dve.tensor_tensor(sp[2], sp[2], sp[4], ALU.add).then_inc(S["p_tap"], 1)
                dve.wait_ge(S["p_tap"], 4)
                dve.tensor_tensor(sp[2], sp[2], sp[1], ALU.mult).then_inc(S["p_tap"], 1)
                dve.wait_ge(S["p_tap"], 5)
                dve.scalar_tensor_tensor(sp[0], sp[0], 0.0, sp[2], ALU.max, ALU.add).then_inc(S["p_tap"], 1)
                dve.wait_ge(S["p_tap"], 6)
                dve.scalar_tensor_tensor(gdec[:], sp[3], -1.0, sp[0], ALU.mult, ALU.mult).then_inc(S["p_tap"], 1)
                dve.tensor_copy(coef[:, :, DT:DT + SH], sp[0][:, :, GH:NH]).then_inc(S["h_v"], 1)
                dve.wait_ge(S["p_tap"], 7)
                dve.tensor_tensor(sgm, bc1(gdec[0:TS, NT, :], TS, SB, NH), bc(seqcol[:], TS, SB, NH), ALU.mult).then_inc(S["h_v"], 1)
                dve.tensor_scalar(coef[:, :, BETA:BETA + GH], coef[:, :, BETA:BETA + GH], 1.0, None, ALU.add).then_inc(S["p_tap"], 1)
                dve.wait_ge(S["p_tap"], 8)
                dve.reciprocal(coef[:, :, BETA:BETA + GH], coef[:, :, BETA:BETA + GH]).then_inc(S["h_v"], 1)
                dve.wait_ge(S["h_v"], 7)
                dve.wait_ge(S["h_a"], 10)
                dve.scalar_tensor_tensor(coef[:, :, NBEG:NBEG + GH], coef[:, :, BETA:BETA + GH], -1.0, coef[:, :, EGAM:EGAM + GH], ALU.mult, ALU.mult)
                dve.tensor_tensor(coef[:, :, DTE:DTE + SH], coef[:, :, DT:DT + SH], coef[:, :, EREV + GH:EREV + NH], ALU.mult).then_inc(S["h_v"], 1)
                with dve.Fori(0, CT // NW) as j:
                    for r in range(NW):
                        n = NW * j + r
                        dve.wait_ge(S[f"p_state{r}"], 32 * j + 32)
                        dve.tensor_scalar(sample_part(raw[r], 0, CW - 1), past[:, bass.ds(n, 1), :, :].rearrange("p c b s -> p (c b) s"), 1.0, None, ALU.mult).then_inc(S[f"p_past{r}"], 1)
                        dve.wait_ge(S[f"p_raw{r}"], j + 2)
                        dve.wait_ge(S[f"p_past{r}"], j + 1)
                        dve.wait_ge(S[f"p_store{r}"], 32 * j + 32)
                        aP, aS = acc[r][:, 0:TP], acc[r][:, TP:T].rearrange("p (b s) -> p b s", b=SB)
                        w = [convw[:, bass.ds(n, 1), i:i + 1].rearrange("p c i -> p (c i)") for i in range(CW)]
                        cb = convb[:, bass.ds(n, 1)]
                        base = 8 + NW * 3 * j + 3 * r
                        dve.tensor_scalar(aP, raw[r][:, 0:TP], w[0], cb, ALU.mult, ALU.add)
                        dve.tensor_scalar(aS, sample_part(raw[r], 0, SL), w[0], cb, ALU.mult, ALU.add).then_inc(S["p_tap"], 1)
                        for i in range(1, CW):
                            dve.wait_ge(S["p_tap"], base + i)
                            dve.scalar_tensor_tensor(aP, raw[r][:, i:i + TP], w[i], aP, ALU.mult, ALU.add)
                            last = dve.scalar_tensor_tensor(aS, sample_part(raw[r], i, SL), w[i], aS, ALU.mult, ALU.add)
                            last.then_inc(S["p_tap"] if i < CW - 1 else S[f"p_conv{r}"], 1)
                        dve.wait_ge(S[f"p_exp{r}"], j + 1)
                        dve.tensor_scalar(eneg[r], eneg[r], 1.0, None, ALU.add).then_inc(S[f"p_one{r}"], 1)
                        dve.wait_ge(S[f"p_one{r}"], j + 1)
                        dve.reciprocal(eneg[r], eneg[r]).then_inc(S[f"p_rec{r}"], 1)
                        dve.wait_ge(S[f"p_rec{r}"], j + 1)
                        dve.tensor_tensor(acc[r], acc[r], eneg[r], ALU.mult).then_inc(S[f"p_silu{r}"], 1)


        next_stage()
        A = Arena()
        cv = A(P, CT, C)
        xTs = A(P, KT, C)
        wz = A(P, KT, D)
        wo = A(P, KT, D)
        wr = A(P, KT, EG + E)
        hrow = A(P, 2, 512)
        srow = A(P, SH)
        cf = A(C, NCF)
        cg = A(C, NH)
        ge = A(P, NH)
        St = A(P, GH, DK)
        Ht = A(P, SH * SP_)
        k_tok = A(C, GH, DK)
        x_tok = A(C, SH, SP_)
        b_tok = A(C, SG, SN)
        q2 = A(P, GH * C)
        sq = A(C, 512)
        rs = A(C, 8)
        rp = A(C, 8)
        khat = k_tok
        kb = A(C, GH, DK)
        kgn = A(C, GH, DK)
        kd = A(C, GH, DK)
        vb = A(C, GH, DK)
        xdt = A(C, SH, SP_)
        xdte = A(C, SH, SP_)
        gm = A(C, NH, C)
        dm = A(C, NH, C)
        khatT = A(P, GH * C)
        kbT = A(P, GH * C)
        at = A(C, GH, C)
        bt = [A(C, GH, C) for _ in range(2)]
        qkm = A(C, GH, C)
        cbd = A(C, SH, C)
        th = A(C, 2, 512)
        sz = th
        X = A(C, GH, C)
        XT = A(C, GH, C)
        ys = A(C, GH, C)
        wt = A(P, GH * C)
        u = A(C, GH, DK)
        o = A(C, GH, DK)
        y = A(C, 512)
        os_ = A(C, 8)
        op_ = A(C, 8)
        mixed = sz
        mixT = A(P, KT, C)
        res = A(C, D)
        st6 = A(C, 2, 6)
        mv = A(C, 2)
        rstd = A(C, 4)
        x1 = A(C, D)
        x1T = mixT

        zero = A(P, P)
        chunk_sems = [
            "k_tok", "x_tok", "b_tok", "q2", "ksq", "rs", "rse", "rp", "khat", "kb", "kgn", "kd", "vb", "xdt", "xdte",
            "cf", "gm", "dexp", "dm", "khatT", "kbT", "at", "a0", "qkm", "cbd", "tanh", "sz", "sza", "szb", "x0",
            "wt", "u", "o1", "o2", "osq", "oss", "osm", "opw", "of", "on", "mixa", "y1", "y2", "y3", "y4", "y5", "ysq",
            "mixb", "sdec", "snew", "hdec", "hnew", "mixT", "res", "stat", "mv", "mve", "rstd", "nmr", "xn", "xg", "x1", "x1T", "rlog",
            "kT_ps", "vT_ps", "xT_ps", "bq_ps", "cb_ps", "d_ps", "kk_ps", "z_ps", "kkqk_ps", "a0_ps", "wt_ps", "u_ps",
            "qs_ps", "o_ps", "s_ps", "ys_ps", "h_ps", "mt_ps", "out_ps", "x1t_ps", "lg_ps"]
        sem(*chunk_sems)
        sem("z_st", "m_const", "m_zero", "l_cv", "l_xt", "l_xr", "x1_st", "lv_bt", "lv_y", "lv_ysb", "lv_z", "lv_x", "s_misc")
        NL = LEVELS - 1

        def cfg(sample):
            n = TS if sample else C
            return n, (smask if sample else mask)

        def tile_tensor(e, i, n1, sample):
            n, mk = cfg(sample)
            nl = (SLEVELS if sample else LEVELS) - 1

            def fm(t, h):
                return t[:, h * n:(h + 1) * n]

            e.wait_ge(S["l_cv"], 16 * n1)
            e.wait_ge(S["rlog"], i + 1)
            e.wait_ge(S["hnew"], i + 1)
            e.wait_ge(S["snew"], i + 1)
            for h in range(GH):
                last = e.transpose(bank[0][0:n, h * P:(h + 1) * P], cv[:, 4 + h, 0:n], ident[:])
            last.then_inc(S["kT_ps"], 1)
            for h in range(GH):
                last = e.transpose(bank[1][0:n, h * P:(h + 1) * P], cv[:, 8 + h, 0:n], ident[:])
            last.then_inc(S["vT_ps"], 1)
            for h in range(GH):
                last = e.transpose(bank[2][0:n, h * P:(h + 1) * P], cv[:, 12 + h, 0:n], ident[:])
            last.then_inc(S["xT_ps"], 1)
            for g in range(SG):
                e.transpose(bank[3][0:n, g * P:(g + 1) * P], cv[:, 16 + g, 0:n], ident[:])
            e.wait_ge(S["q2"], n1)
            for h in range(GH):
                last = e.matmul(bank[3][0:n, 256 + h:257 + h], fm(q2, h), ones[:, 0:1], start=True, stop=True)
            last.then_inc(S["bq_ps"], 1)
            for g in range(SG):
                last = e.matmul(bank[4][0:n, g * n:(g + 1) * n], cv[:, 16 + g, 0:n], cv[:, 18 + g, 0:n], start=True, stop=True)
            last.then_inc(S["cb_ps"], 1)
            e.wait_ge(S["gm"], n1 + 1)
            for d in range(3):
                last = e.matmul(bank[5 + d][0:n, 0:4 * n], mk[0:n, GT, 0:n],
                                gm[0:n, 4 * d:4 * (d + 1), 0:n], start=True, stop=True)
            last.then_inc(S["d_ps"], 1)
            e.wait_ge(S["l_xt"], 16 * n1)
            e.wait_ge(S["x_tok"], n1)
            e.wait_ge(S["b_tok"], n1)
            e.wait_ge(S["rs"], n1)
            for s in range(2):
                for k in range(KT):
                    last = e.matmul(bank[2 + s][0:n, :], xTs[:, k, 0:n], wz[:, k, s * 512:(s + 1) * 512],
                                    start=(k == 0), stop=(k == KT - 1))
            last.then_inc(S["z_ps"], 1)
            e.wait_ge(S["khat"], n1)
            e.wait_ge(S["kb"], n1)
            e.wait_ge(S["k_tok"], n1)
            e.wait_ge(S["vb"], n1)
            for h in range(GH):
                e.transpose(bank[0][:, h * n:(h + 1) * n], khat[0:n, h, :], ident[0:n, 0:n])
            for h in range(GH):
                last = e.transpose(bank[1][:, h * n:(h + 1) * n], kb[0:n, h, :], ident[0:n, 0:n])
            last.then_inc(S["kk_ps"], 1)
            e.wait_ge(S["khatT"], n1)
            e.wait_ge(S["kbT"], n1)
            e.wait_ge(S["cbd"], n1 + 1)
            e.wait_ge(S["dexp"], n1)
            for h in range(GH):
                e.matmul(bank[4][0:n, h * n:(h + 1) * n], fm(khatT, h), fm(kbT, h), start=True, stop=True)
            for h in range(GH):
                last = e.matmul(bank[5][0:n, h * n:(h + 1) * n], fm(khatT, h), cv[:, h, 0:n], start=True, stop=True)
            last.then_inc(S["kkqk_ps"], 1)
            e.wait_ge(S["a0"], n1)
            for h in range(GH):
                last = e.transpose(bank[6][0:n, h * n:(h + 1) * n], bt[0][0:n, h, 0:n], ident[0:n, 0:n])
            last.then_inc(S["a0_ps"], 1)
            e.wait_ge(S["x0"], n1)
            for l in range(1, nl + 1):
                cnt = NL * i + l
                e.wait_ge(S["lv_bt"], cnt)
                if l > 1:
                    e.wait_ge(S["lv_x"], cnt - 1)
                for h in range(GH):
                    last = e.matmul(bank[0][0:n, h * n:(h + 1) * n], bt[l % 2][0:n, h, 0:n], X[0:n, h, 0:n], start=True, stop=True)
                last.then_inc(S["lv_y"], 1)
                e.wait_ge(S["lv_ysb"], cnt)
                for h in range(GH):
                    e.matmul(bank[1][0:n, h * n:(h + 1) * n], XT[0:n, h, 0:n], ys[0:n, h, 0:n], start=True, stop=True)
                for h in range(GH):
                    last = e.matmul(bank[7][0:n, h * n:(h + 1) * n], ys[0:n, h, 0:n], XT[0:n, h, 0:n], start=True, stop=True)
                last.then_inc(S["lv_z"], 1)
            e.wait_ge(S["lv_x"], NL * i + nl)
            e.wait_ge(S["kgn"], n1 + 1)
            e.wait_ge(S["at"], n1 + 1)
            for h in range(GH):
                last = e.matmul(bank[4][:, h * n:(h + 1) * n], kgn[0:n, h, :], XT[0:n, h, 0:n], start=True, stop=True)
            last.then_inc(S["wt_ps"], 1)
            if sample:
                sample_tensor(e, n1, n)
            else:
                for h in range(GH):
                    last = e.matmul(bank[6][0:n, h * P:(h + 1) * P], cv[:, h, 0:n], St[:, h, :], start=True, stop=True)
                last.then_inc(S["qs_ps"], 1)
                e.wait_ge(S["wt"], n1)
                e.wait_ge(S["qkm"], n1 + 1)
                for h in range(GH):
                    e.matmul(bank[5][0:n, h * P:(h + 1) * P], XT[0:n, h, 0:n], vb[0:n, h, :], start=True, stop=False)
                    last = e.matmul(bank[5][0:n, h * P:(h + 1) * P], fm(wt, h), St[:, h, :], start=False, stop=True)
                last.then_inc(S["u_ps"], 1)
                e.wait_ge(S["u"], n1)
                for h in range(GH):
                    last = e.matmul(bank[0][0:n, h * P:(h + 1) * P], qkm[0:n, h, 0:n], u[0:n, h, :], start=True, stop=True)
                last.then_inc(S["o_ps"], 1)
                e.wait_ge(S["kd"], n1 + 1)
                for h in range(GH):
                    last = e.matmul(bank[1][:, h * P:(h + 1) * P], kd[0:n, h, :], u[0:n, h, :], start=True, stop=True)
                last.then_inc(S["s_ps"], 1)
                e.wait_ge(S["sz"], n1)
                e.wait_ge(S["xdt"], n1)
                e.wait_ge(S["xdte"], n1 + 1)
                for g in range(SG):
                    e.matmul(bank[2][0:n, g * 256:(g + 1) * 256], cv[:, 18 + g, 0:n], Ht[:, g * 256:(g + 1) * 256], start=True, stop=True)
                for h in range(SH):
                    last = e.matmul(bank[3][0:n, h * SP_:(h + 1) * SP_], cbd[0:n, h, 0:n], xdt[0:n, h, :], start=True, stop=True)
                last.then_inc(S["ys_ps"], 1)
                e.wait_ge(S["wt"], n1)
                for g in range(SG):
                    last = e.matmul(bank[4][:, g * 256:(g + 1) * 256], b_tok[0:n, g, :], xdte[0:n].rearrange("p h d -> p (h d)")[:, g * 256:(g + 1) * 256],
                                    start=True, stop=True)
                last.then_inc(S["h_ps"], 1)
            e.wait_ge(S["mixa"], n1)
            e.wait_ge(S["mixb"], n1 + 1)
            e.wait_ge(S["u"], n1)
            e.wait_ge(S["o1"], n1)
            for k in range(KT):
                b_, q_ = 5 + k // 4, k % 4
                last = e.transpose(bank[b_][:, q_ * n:(q_ + 1) * n], mixed[0:n, k // 4, q_ * P:(q_ + 1) * P], ident[0:n, 0:n])
            last.then_inc(S["mt_ps"], 1)
            e.wait_ge(S["mixT"], n1)
            e.wait_ge(S["o2"], n1 + 1)
            for s in range(2):
                for k in range(KT):
                    last = e.matmul(bank[7 if s == 0 else 0][0:n, :], mixT[:, k, 0:n], wo[:, k, s * 512:(s + 1) * 512],
                                    start=(k == 0), stop=(k == KT - 1))
            last.then_inc(S["out_ps"], 1)
            e.wait_ge(S["x1"], n1)
            e.wait_ge(S["y1"], n1 + 1)
            if not sample:
                e.wait_ge(S["snew"], n1 + 1)
            for k in range(KT):
                b_, q_ = 1 + k // 4, k % 4
                last = e.transpose(bank[b_][:, q_ * n:(q_ + 1) * n], x1[0:n, k * P:(k + 1) * P], ident[0:n, 0:n])
            last.then_inc(S["x1t_ps"], 1)
            e.wait_ge(S["x1T"], n1)
            e.wait_ge(S["y2"], n1)
            for k in range(KT):
                last = e.matmul(bank[3][0:n, 0:EG + E], x1T[:, k, 0:n], wr[:, k, :], start=(k == 0), stop=(k == KT - 1))
            last.then_inc(S["lg_ps"], 1)

        def tile_scalar(e, i, n1, sample):
            n, mk = cfg(sample)
            nl = (SLEVELS if sample else LEVELS) - 1
            e.wait_ge(S["l_cv"], 16 * n1)
            e.wait_ge(S["o2"], i + 1)
            e.activation(q2[:, 0:GH * n].rearrange("p (h n) -> p h n", n=n), cv[:, 0:GH, 0:n], ACT.Square).then_inc(S["q2"], 1)
            e.wait_ge(S["kT_ps"], n1)
            e.wait_ge(S["kd"], i + 1)
            e.activation(k_tok[0:n].rearrange("p h d -> p (h d)"), bank[0][0:n, :], ACT.Copy).then_inc(S["k_tok"], 1)
            e.wait_ge(S["xT_ps"], n1)
            e.wait_ge(S["y4"], i + 1)
            e.activation(x_tok[0:n].rearrange("p h d -> p (h d)"), bank[2][0:n, :], ACT.Copy).then_inc(S["x_tok"], 1)
            e.wait_ge(S["bq_ps"], n1)
            e.activation(b_tok[0:n].rearrange("p h d -> p (h d)"), bank[3][0:n, 0:256], ACT.Copy).then_inc(S["b_tok"], 1)
            e.wait_ge(S["d_ps"], n1 + 1)
            e.wait_ge(S["cbd"], i + 1)
            e.wait_ge(S["qkm"], i + 1)
            e.wait_ge(S["at"], i + 1)
            for d in range(3):
                last = e.activation(dm[0:n, 4 * d:4 * d + 4, 0:n], bank[5 + d][0:n, 0:4 * n].rearrange("p (h n) -> p h n", n=n), ACT.Exp)
            last.then_inc(S["dexp"], 1)
            e.wait_ge(S["kk_ps"], n1)
            e.activation(khatT[:, 0:GH * n], bank[0][:, 0:GH * n], ACT.Copy).then_inc(S["khatT"], 1)
            e.activation(kbT[:, 0:GH * n], bank[1][:, 0:GH * n], ACT.Copy).then_inc(S["kbT"], 1)
            e.wait_ge(S["z_ps"], n1 + 1)
            e.wait_ge(S["mt_ps"], i + 1)
            for s in range(2):
                last = e.activation(th[0:n, s, :], bank[2 + s][0:n, :], ACT.Tanh, scale=0.5)
            last.then_inc(S["tanh"], 1)
            for l in range(1, nl + 1):
                cnt = NL * i + l
                e.wait_ge(S["lv_y"], cnt)
                e.activation(ys[0:n, :, 0:n], bank[0][0:n, 0:GH * n].rearrange("p (h n) -> p h n", n=n), ACT.Copy).then_inc(S["lv_ysb"], 1)
            e.wait_ge(S["wt_ps"], n1)
            e.activation(wt[:, 0:GH * n], bank[4][:, 0:GH * n], ACT.Copy).then_inc(S["wt"], 1)
            e.wait_ge(S["u_ps"], n1)
            e.activation(u[0:n].rearrange("p h d -> p (h d)"), bank[5][0:n, :], ACT.Copy).then_inc(S["u"], 1)
            e.wait_ge(S["mt_ps"], n1 + 1)
            for s in range(2):
                last = e.activation(mixT[:, 4 * s:4 * s + 4, 0:n], bank[5 + s][:, 0:4 * n].rearrange("p (k n) -> p k n", n=n), ACT.Copy)
            last.then_inc(S["mixT"], 1)
            e.wait_ge(S["nmr"], n1)
            e.activation(res[0:n, :], res[0:n, :], ACT.Identity, bias=rstd[0:n, 2:3], scale=rstd[0:n, 1:2]).then_inc(S["xn"], 1)
            e.wait_ge(S["x1t_ps"], n1 + 1)
            for s in range(2):
                last = e.activation(x1T[:, 4 * s:4 * s + 4, 0:n], bank[1 + s][:, 0:4 * n].rearrange("p (k n) -> p k n", n=n), ACT.Copy)
            last.then_inc(S["x1T"], 1)

        def tile_vector(e, i, n1, sample):
            n, mk = cfg(sample)
            nl = (SLEVELS if sample else LEVELS) - 1
            e.wait_ge(S["gm"], i + 1)
            e.wait_ge(S["xdte"], i + 1)
            e.wait_ge(S["kd"], i + 1)
            e.wait_ge(S["kgn"], i + 1)
            e.wait_ge(S["hdec"], i + 1)
            e.wait_ge(S["mixb"], i + 1)
            e.wait_ge(S["y1"], i + 1)
            if sample:
                e.tensor_scalar(cf[0:n], coef[0:n, NT, :], 1.0, None, ALU.mult)
                e.tensor_scalar(cg[0:n], gdec[0:n, NT, :], 1.0, None, ALU.mult).then_inc(S["cf"], 1)
            else:
                e.tensor_scalar(cf[:], coef[:, bass.ds(i, 1), :].rearrange("p t c -> p (t c)"), 1.0, None, ALU.mult)
                e.tensor_scalar(ge[:], gend[:, bass.ds(i, 1), :].rearrange("p t c -> p (t c)"), 1.0, None, ALU.mult)
                e.tensor_scalar(cg[:], gdec[:, bass.ds(i, 1), :].rearrange("p t c -> p (t c)"), 1.0, None, ALU.mult).then_inc(S["cf"], 1)
            e.wait_ge(S["cf"], n1)
            e.wait_ge(S["k_tok"], n1)
            k2, kh = k_tok[0:n], khat[0:n]
            e.tensor_tensor(sq[0:n].rearrange("p (h d) -> p h d", h=GH), k2, k2, ALU.mult).then_inc(S["ksq"], 1)
            e.wait_ge(S["vT_ps"], n1)
            e.tensor_tensor(vb[0:n], bank[1][0:n, :].rearrange("p (h d) -> p h d", h=GH), bc(cf[0:n, BETA:BETA + GH], n, GH, DK), ALU.mult).then_inc(S["vb"], 1)
            e.wait_ge(S["ksq"], n1)
            e.tensor_reduce(rs[0:n, 0:4], sq[0:n].rearrange("p (h d) -> p h d", h=GH), AX, ALU.add)
            e.wait_ge(S["b_tok"], n1)
            e.tensor_copy(rs[0:n, 4:8], bank[3][0:n, 256:260]).then_inc(S["rs"], 1)
            e.wait_ge(S["rs"], n1)
            e.tensor_scalar(rs[0:n], rs[0:n], EPS, None, ALU.add).then_inc(S["rse"], 1)
            e.wait_ge(S["rp"], n1)
            e.tensor_tensor(kh, k2, bc(rp[0:n, 0:4], n, GH, DK), ALU.mult).then_inc(S["khat"], 1)
            e.wait_ge(S["khat"], n1)
            e.tensor_tensor(kb[0:n], kh, bc(cf[0:n, BETA:BETA + GH], n, GH, DK), ALU.mult).then_inc(S["kb"], 1)
            e.wait_ge(S["cb_ps"], n1)
            e.wait_ge(S["dm"], n1)
            for g in range(SG):
                last = e.tensor_tensor(cbd[0:n, 4 * g:4 * g + 4, 0:n], dm[0:n, GH + 4 * g:GH + 4 * g + 4, 0:n],
                                       bc1(bank[4][0:n, g * n:(g + 1) * n], n, 4, n), ALU.mult)
            last.then_inc(S["cbd"], 1)
            e.wait_ge(S["kkqk_ps"], n1 + 1)
            e.tensor_tensor(at[0:n, :, 0:n], bank[4][0:n, 0:GH * n].rearrange("p (h n) -> p h n", n=n), dm[0:n, 0:GH, 0:n], ALU.mult).then_inc(S["at"], 1)
            e.tensor_tensor(qkm[0:n, :, 0:n], bank[5][0:n, 0:GH * n].rearrange("p (h n) -> p h n", n=n), dm[0:n, 0:GH, 0:n], ALU.mult).then_inc(S["qkm"], 1)
            e.wait_ge(S["at"], n1 + 1)
            e.tensor_tensor(bt[0][0:n, :, 0:n], at[0:n, :, 0:n], bc1(mk[0:n, LV, 0:n], n, GH, n), ALU.mult).then_inc(S["a0"], 1)
            e.wait_ge(S["a0"], n1)
            idn = bc1(ident[0:n, 0:n], n, GH, n)
            e.tensor_tensor(XT[0:n, :, 0:n], idn, bt[0][0:n, :, 0:n], ALU.subtract)
            e.wait_ge(S["a0_ps"], n1)
            e.tensor_tensor(X[0:n, :, 0:n], idn, bank[6][0:n, 0:GH * n].rearrange("p (h n) -> p h n", n=n), ALU.subtract).then_inc(S["x0"], 1)
            e.wait_ge(S["tanh"], n1)
            for s in range(2):
                last = e.scalar_tensor_tensor(sz[0:n, s, :], th[0:n, s, :], 1.0, bank[2 + s][0:n, :], ALU.add, ALU.mult)
            last.then_inc(S["sz"], 1)
            for l in range(1, nl + 1):
                cnt = NL * i + l
                e.wait_ge(S["lv_z"], cnt)
                e.wait_ge(S["x0"], n1)
                if l > 1:
                    e.wait_ge(S["lv_x"], cnt - 1)
                e.tensor_tensor(X[0:n, :, 0:n], X[0:n, :, 0:n], bank[1][0:n, 0:GH * n].rearrange("p (h n) -> p h n", n=n), ALU.subtract)
                e.tensor_tensor(XT[0:n, :, 0:n], XT[0:n, :, 0:n], bank[7][0:n, 0:GH * n].rearrange("p (h n) -> p h n", n=n), ALU.subtract).then_inc(S["lv_x"], 1)
            if sample:
                e.wait_ge(S["z_ps"], n1 + 1)
                for h in range(GH):
                    last = e.tensor_tensor(qm[:, h], bc1(cv[:, h, 0:TS], P, SB, TS), seqrow[:], ALU.mult)
                last.then_inc(S["ss_qm"], 1)
                e.wait_ge(S["wt"], n1)
                for h in range(GH):
                    last = e.tensor_tensor(wm[:, h], bc1(wt[:, h * n:(h + 1) * n], P, SB, TS), seqrow[:], ALU.mult)
                last.then_inc(S["ss_wm"], 1)
            o3, y3 = o[0:n], y[0:n].rearrange("p (h d) -> p h d", h=SH)
            e.wait_ge(S["qs_ps"], n1 + 1)
            e.tensor_tensor(o3, bank[6][0:n, :].rearrange("p (h d) -> p h d", h=GH), bc(cf[0:n, EGAM:EGAM + GH], n, GH, DK), ALU.mult).then_inc(S["o1"], 1)
            e.wait_ge(S["o_ps"], n1)
            e.wait_ge(S["o1"], n1)
            e.tensor_tensor(o3, o3, bank[0][0:n, :].rearrange("p (h d) -> p h d", h=GH), ALU.add).then_inc(S["o2"], 1)
            if not sample:
                e.wait_ge(S["s_ps"], n1)
                e.wait_ge(S["sdec"], n1)
                e.tensor_tensor(St, St, bank[1][:].rearrange("p (h d) -> p h d", h=GH), ALU.add).then_inc(S["snew"], 1)
            else:
                sample_vector_state(e, n1, n)
            e.wait_ge(S["ys_ps"], n1 + 1)
            e.tensor_tensor(y3, bank[2][0:n, :].rearrange("p (h d) -> p h d", h=SH), bc(cf[0:n, EGAM + GH:EGAM + NH], n, SH, SP_), ALU.mult).then_inc(S["y1"], 1)
            e.wait_ge(S["y1"], n1 + 1)
            e.tensor_tensor(y[0:n], y[0:n], bank[3][0:n, :], ALU.add).then_inc(S["y2"], 1)
            if not sample:
                e.wait_ge(S["h_ps"], n1 + 1)
                e.wait_ge(S["hdec"], n1 + 1)
                e.tensor_tensor(Ht, Ht, bank[4][:], ALU.add).then_inc(S["hnew"], 1)
            e.wait_ge(S["o2"], n1 + 1)
            e.tensor_tensor(sq[0:n], o3.rearrange("p h d -> p (h d)"), o3.rearrange("p h d -> p (h d)"), ALU.mult).then_inc(S["osq"], 1)
            e.wait_ge(S["osq"], n1)
            e.wait_ge(S["y2"], n1)
            e.wait_ge(S["y3"], n1)
            e.tensor_reduce(os_[0:n, 0:4], sq[0:n].rearrange("p (h d) -> p h d", h=GH), AX, ALU.add).then_inc(S["oss"], 1)
            e.tensor_tensor(y3, y3, x_tok[0:n], ALU.add).then_inc(S["y4"], 1)
            e.wait_ge(S["oss"], n1)
            e.tensor_tensor(os_[0:n, 0:4], os_[0:n, 0:4], rp[0:n, 4:8], ALU.mult).then_inc(S["s_misc"], 1)
            e.wait_ge(S["s_misc"], 4 * i + 1)
            e.tensor_tensor(os_[0:n, 0:4], os_[0:n, 0:4], rp[0:n, 4:8], ALU.mult).then_inc(S["s_misc"], 1)
            e.wait_ge(S["y4"], n1 + 1)
            e.tensor_tensor(y[0:n], y[0:n], sz[0:n, 1, :], ALU.mult).then_inc(S["y5"], 1)
            e.wait_ge(S["s_misc"], 4 * i + 2)
            e.tensor_scalar(os_[0:n, 0:4], os_[0:n, 0:4], 1.0 / (DK * DK), EPS, ALU.mult, ALU.add)
            e.wait_ge(S["y5"], n1)
            e.tensor_tensor(sq[0:n], y[0:n], y[0:n], ALU.mult).then_inc(S["ysq"], 1)
            e.wait_ge(S["ysq"], n1)
            e.tensor_reduce(os_[0:n, 4:6], sq[0:n].rearrange("p (g d) -> p g d", g=SG), AX, ALU.add).then_inc(S["s_misc"], 1)
            e.wait_ge(S["s_misc"], 4 * i + 3)
            e.tensor_scalar(os_[0:n, 4:6], os_[0:n, 4:6], 1.0 / (4 * 256), EPS, ALU.mult, ALU.add).then_inc(S["osm"], 1)
            e.wait_ge(S["opw"], n1)
            e.scalar_tensor_tensor(op_[0:n, 0:4], op_[0:n, 0:4], 0.5 * DK ** -0.5, rp[0:n, 4:8], ALU.mult, ALU.mult)
            e.tensor_scalar(op_[0:n, 4:6], op_[0:n, 4:6], 0.5, None, ALU.mult).then_inc(S["of"], 1)
            e.wait_ge(S["of"], n1)
            e.tensor_tensor(o3, o3, bc(op_[0:n, 0:4], n, GH, DK), ALU.mult).then_inc(S["on"], 1)
            yg = y[0:n].rearrange("p (g d) -> p g d", g=SG)
            e.tensor_tensor(yg, yg, bc(op_[0:n, 4:6], n, SG, 256), ALU.mult).then_inc(S["s_misc"], 1)
            e.wait_ge(S["on"], n1)
            e.wait_ge(S["sza"], n1)
            e.tensor_tensor(mixed[0:n, 0, :], o3.rearrange("p h d -> p (h d)"), sz[0:n, 0, :], ALU.mult).then_inc(S["mixa"], 1)
            e.wait_ge(S["l_xr"], 16 * n1)
            e.wait_ge(S["out_ps"], n1)
            for s in range(2):
                last = e.scalar_tensor_tensor(res[0:n, s * 512:(s + 1) * 512], res[0:n, s * 512:(s + 1) * 512], ALPHA,
                                              bank[7 if s == 0 else 0][0:n, :], ALU.mult, ALU.add)
            last.then_inc(S["res"], 1)
            e.wait_ge(S["res"], n1)
            for s in range(2):
                last = e.bn_stats(st6[0:n, s, :], res[0:n, s * 512:(s + 1) * 512])
            last.then_inc(S["stat"], 1)
            e.wait_ge(S["m_zero"], 1)
            e.wait_ge(S["stat"], n1)
            e.bn_aggr(mv[0:n], st6[0:n].rearrange("p a b -> p (a b)")).then_inc(S["mv"], 1)
            e.wait_ge(S["mv"], n1)
            e.tensor_scalar(rstd[0:n, 0:1], mv[0:n, 1:2], EPS, None, ALU.add).then_inc(S["mve"], 1)
            e.wait_ge(S["rstd"], n1)
            e.scalar_tensor_tensor(rstd[0:n, 2:3], mv[0:n, 0:1], -1.0, rstd[0:n, 1:2], ALU.mult, ALU.mult).then_inc(S["nmr"], 1)
            e.wait_ge(S["xg"], n1 + 1)
            e.wait_ge(S["x1_st"], 16 * i + 16)
            e.tensor_tensor(x1[0:n], x1[0:n], lnrow[0:n, 1, :], ALU.add).then_inc(S["x1"], 1)
            e.wait_ge(S["lg_ps"], n1)
            if sample:
                e.tensor_scalar(rlog[0:n, NT, :], bank[3][0:n, 0:EG + E], 1.0, None, ALU.mult).then_inc(S["rlog"], 1)
            else:
                e.tensor_scalar(rlog[:, bass.ds(i, 1), :].rearrange("p t c -> p (t c)"), bank[3][0:n, 0:EG + E], 1.0, None, ALU.mult).then_inc(S["rlog"], 1)

        def tile_gpsimd(e, i, n1, sample):
            n, mk = cfg(sample)
            nl = (SLEVELS if sample else LEVELS) - 1
            e.wait_ge(S["cf"], n1)
            e.wait_ge(S["d_ps"], i + 1)
            e.tensor_tensor(gm[0:n, :, 0:n], bc1(mk[0:n, INC, 0:n], n, NH, n), bc(cg[0:n], n, NH, n), ALU.mult).then_inc(S["gm"], 1)
            e.wait_ge(S["rse"], n1)
            e.tensor_tensor(rp[0:n], rs[0:n], mhalf[0:n, 0:8], ALU.pow).then_inc(S["rp"], 1)
            e.wait_ge(S["x_tok"], n1)
            e.wait_ge(S["ys_ps"], i + 1)
            e.wait_ge(S["h_ps"], i + 1)
            x3 = x_tok[0:n]
            e.tensor_tensor(xdt[0:n], x3, bc(cf[0:n, DT:DT + SH], n, SH, SP_), ALU.mult).then_inc(S["xdt"], 1)
            e.tensor_tensor(xdte[0:n], x3, bc(cf[0:n, DTE:DTE + SH], n, SH, SP_), ALU.mult).then_inc(S["xdte"], 1)
            e.wait_ge(S["dexp"], n1)
            e.tensor_tensor(dm[0:n, :, 0:n], dm[0:n, :, 0:n], bc1(mk[0:n, INC, 0:n], n, NH, n), ALU.mult).then_inc(S["dm"], 1)
            e.wait_ge(S["khat"], n1)
            e.tensor_tensor(kgn[0:n], khat[0:n], bc(cf[0:n, NBEG:NBEG + GH], n, GH, DK), ALU.mult).then_inc(S["kgn"], 1)
            e.tensor_tensor(kd[0:n], khat[0:n], bc(cf[0:n, EREV:EREV + GH], n, GH, DK), ALU.mult).then_inc(S["kd"], 1)
            e.wait_ge(S["at"], n1 + 1)
            for l in range(1, nl + 1):
                cnt = NL * i + l
                if l == 2:
                    e.wait_ge(S["a0_ps"], n1)
                    e.wait_ge(S["x0"], n1)
                if l > 2:
                    e.wait_ge(S["lv_y"], cnt - 2)
                e.tensor_tensor(bt[l % 2][0:n, :, 0:n], at[0:n, :, 0:n], bc1(mk[0:n, LV + l, 0:n], n, GH, n), ALU.mult).then_inc(S["lv_bt"], 1)
            if not sample:
                e.wait_ge(S["qs_ps"], n1 + 1)
                e.wait_ge(S["u_ps"], n1)
                e.tensor_tensor(St, St, bc(ge[:, 0:GH], P, GH, DK), ALU.mult).then_inc(S["sdec"], 1)
            e.wait_ge(S["xdte"], n1 + 1)
            e.tensor_tensor(x3, x3, bc(srow[0:n], n, SH, SP_), ALU.mult).then_inc(S["y3"], 1)
            e.wait_ge(S["sz"], n1)
            e.tensor_tensor(sz[0:n, 0, :], sz[0:n, 0, :], hrow[0:n, 0, :], ALU.mult).then_inc(S["sza"], 1)
            if not sample:
                e.wait_ge(S["ys_ps"], n1 + 1)
                e.tensor_tensor(Ht.rearrange("p (h d) -> p h d", h=SH), Ht.rearrange("p (h d) -> p h d", h=SH), bc(ge[:, GH:NH], P, SH, SP_), ALU.mult).then_inc(S["hdec"], 1)
            else:
                sample_gpsimd(e, n1, n)
            e.wait_ge(S["osm"], n1)
            e.tensor_tensor(op_[0:n, 0:6], os_[0:n, 0:6], mhalf[0:n, 0:6], ALU.pow).then_inc(S["opw"], 1)
            e.wait_ge(S["s_misc"], 4 * n1)
            e.tensor_tensor(mixed[0:n, 1, :], y[0:n], hrow[0:n, 1, :], ALU.mult).then_inc(S["mixb"], 1)
            e.wait_ge(S["mve"], n1)
            e.tensor_tensor(rstd[0:n, 1:2], rstd[0:n, 0:1], mhalf[0:n, 0:1], ALU.pow).then_inc(S["rstd"], 1)
            e.wait_ge(S["xn"], n1)
            e.wait_ge(S["x1_st"], 16 * i + 16)
            e.wait_ge(S["x1t_ps"], i + 1)
            e.tensor_tensor(x1[0:n], res[0:n], lnrow[0:n, 0, :], ALU.mult).then_inc(S["xg"], 1)

        sem("ss_in", "sh_in", "ss_wm", "ss_qm", "ss_cm", "ss_um", "ss_ps", "ss_dec", "ss_new", "sh_xm", "sh_ps", "sh_dec", "sh_new", "p_out")
        Ss = A(P, SB, GH, DK)
        um = [t[0:TS, 0:SB * DK].rearrange("p (b d) -> p b d", b=SB) for t in (gm.rearrange("p h n -> p (h n)"), x1)]
        xm = cv.rearrange("p c n -> p (c n)")[0:TS, 0:SB * 256].rearrange("p (b d) -> p b d", b=SB)
        cmk = A(P, SG, SB, TS)
        wzf = wz.rearrange("p a b -> p (a b)")
        Hs = wzf[:, 0:4096].rearrange("p (b c) -> p b c", b=SB)
        qm = wzf[:, 4096:6144].rearrange("p (h b n) -> p h b n", h=GH, b=SB)
        wm = wzf[:, 6144:8192].rearrange("p (h b n) -> p h b n", h=GH, b=SB)

        def sample_tensor(e, n1, n):
            e.wait_ge(S["ss_qm"], 1)
            e.wait_ge(S["ss_in"], 16)
            for h in range(GH):
                for b in range(SB):
                    last = e.matmul(bank[6][0:n, h * P:(h + 1) * P], qm[:, h, b, :], Ss[:, b, h, :], start=(b == 0), stop=(b == SB - 1))
            last.then_inc(S["qs_ps"], 1)
            e.wait_ge(S["ss_wm"], 1)
            e.wait_ge(S["qkm"], n1 + 1)
            for h in range(GH):
                e.matmul(bank[5][0:n, h * P:(h + 1) * P], XT[0:n, h, 0:n], vb[0:n, h, :], start=True, stop=False)
                for b in range(SB):
                    last = e.matmul(bank[5][0:n, h * P:(h + 1) * P], wm[:, h, b, :], Ss[:, b, h, :], start=False, stop=(b == SB - 1))
            last.then_inc(S["u_ps"], 1)
            e.wait_ge(S["u"], n1)
            for h in range(GH):
                last = e.matmul(bank[0][0:n, h * P:(h + 1) * P], qkm[0:n, h, 0:n], u[0:n, h, :], start=True, stop=True)
            last.then_inc(S["o_ps"], 1)
            e.wait_ge(S["kd"], n1 + 1)
            e.wait_ge(S["o1"], n1)
            for h in range(GH):
                e.wait_ge(S["ss_um"], h + 1)
                if h:
                    e.wait_ge(S["ss_new"], h)
                for s in range(2):
                    last = e.matmul(bank[1 if s == 0 else 7][:, :], kd[0:n, h, :], um[h % 2].rearrange("p a b -> p (a b)")[:, s * 512:(s + 1) * 512], start=True, stop=True)
                last.then_inc(S["ss_ps"], 1)
            e.wait_ge(S["sz"], n1)
            e.wait_ge(S["xdt"], n1)
            e.wait_ge(S["xdte"], n1 + 1)
            e.wait_ge(S["ss_cm"], 1)
            e.wait_ge(S["sh_in"], 16)
            for g in range(SG):
                for b in range(SB):
                    last = e.matmul(bank[2][0:n, g * 256:(g + 1) * 256], cmk[:, g, b, :], Hs[:, b, g * 256:(g + 1) * 256], start=(b == 0), stop=(b == SB - 1))
            for h in range(SH):
                last = e.matmul(bank[3][0:n, h * SP_:(h + 1) * SP_], cbd[0:n, h, 0:n], xdt[0:n, h, :], start=True, stop=True)
            last.then_inc(S["ys_ps"], 1)
            e.wait_ge(S["ss_new"], 4)
            e.wait_ge(S["ss_wm"], 1)
            for r in range(4):
                e.wait_ge(S["sh_xm"], r // 2 + 1)
                if r:
                    e.wait_ge(S["sh_new"], r)
                for s in range(2):
                    last = e.matmul(bank[4 if s == 0 else 7][:, :], b_tok[0:n, r // 2, :],
                                    xm.rearrange("p b d -> p (b d)")[:, (r % 2) * 1024 + s * 512:(r % 2) * 1024 + (s + 1) * 512], start=True, stop=True)
                last.then_inc(S["sh_ps"], 1)
            e.wait_ge(S["sh_new"], 4)

        def sample_vector_state(e, n1, n):
            for h in range(GH):
                e.wait_ge(S["ss_ps"], h + 1)
                e.wait_ge(S["ss_dec"], 1)
                for s in range(2):
                    d = Ss[:, 4 * s:4 * s + 4, h, :]
                    last = e.tensor_tensor(d, d, bank[1 if s == 0 else 7][:].rearrange("p (b d) -> p b d", b=4), ALU.add)
                last.then_inc(S["ss_new"], 1)
            e.wait_ge(S["sh_dec"], 1)
            for r in range(4):
                e.wait_ge(S["sh_ps"], r + 1)
                for s in range(2):
                    b0 = 4 * (r % 2) + 2 * s
                    d = Hs[:, b0:b0 + 2, (r // 2) * 256:(r // 2 + 1) * 256]
                    last = e.tensor_tensor(d, d, bank[4 if s == 0 else 7][:].rearrange("p (b d) -> p b d", b=2), ALU.add)
                last.then_inc(S["sh_new"], 1)

        def sample_gpsimd(e, n1, n):
            for h in range(GH):
                e.wait_ge(S["u"], n1)
                if h == 1:
                    e.wait_ge(S["x1_st"], 16 * NT + 16)
                if h >= 2:
                    e.wait_ge(S["ss_ps"], h - 1)
                e.tensor_tensor(um[h % 2], bc1(u[0:n, h, :], n, SB, DK), bc(seqcol[:], n, SB, DK), ALU.mult).then_inc(S["ss_um"], 1)
                if h == 0:
                    e.wait_ge(S["qs_ps"], n1 + 1)
                    e.wait_ge(S["u_ps"], n1)
                    for b in range(SB):
                        last = e.tensor_tensor(Ss[:, b], Ss[:, b], bc(sgend[:, b, 0:GH], P, GH, DK), ALU.mult)
                    last.then_inc(S["ss_dec"], 1)
            for g in range(SG):
                if g:
                    e.wait_ge(S["sh_ps"], 2)
                e.tensor_tensor(xm, bc1(xdte[0:n, 4 * g:4 * g + 4, :].rearrange("p h d -> p (h d)"), n, SB, 256), bc(seqcol[:], n, SB, 256), ALU.mult).then_inc(S["sh_xm"], 1)
                if g == 0:
                    e.wait_ge(S["ys_ps"], n1 + 1)
                    for b in range(SB):
                        hb = Hs[:, b, :].rearrange("p (h d) -> p h d", h=SH)
                        last = e.tensor_tensor(hb, hb, bc(sgend[:, b, GH:NH], P, SH, SP_), ALU.mult)
                    last.then_inc(S["sh_dec"], 1)

        begin()
        with nc.Block() as block:
            @block.sync
            def _(e):
                for k in range(KT):
                    e.dma_start(wz[:, k, :], a["w_z"][:, k, :]).then_inc(S["m_const"], 16)
                e.dma_start(wr, a["w_router"]).then_inc(S["m_const"], 16)
                e.dma_start(hrow, a["head_rows"]).then_inc(S["m_const"], 16)
                e.dma_start(srow, a["ssd_d"]).then_inc(S["m_const"], 16)
                for k in range(KT):
                    e.dma_start(wo[:, k, :], a["w_out"][:, k, :]).then_inc(S["m_const"], 16)
                e.dma_start(Ss[:], a["state_gdn"]).then_inc(S["ss_in"], 16)
                e.wait_ge(S["m_zero"], 1)
                with e.Fori(0, NT) as i:
                    e.dma_start(a["d_eo"][bass.ds((E + 2 * i) * BLK, 2 * BLK), :].rearrange("(p r) (s c) -> p (r s) c", r=2, c=P),
                                zero.unsqueeze(1).broadcast_to([P, 2 * KT, P])).then_inc(S["z_st"], 16)
                    e.wait_ge(S["qs_ps"], i + 1)
                    e.wait_ge(S["ys_ps"], i + 1)
                    e.wait_ge(S["kkqk_ps"], i + 1)
                    e.dma_start(cv, a["d_conv"][bass.ds(i, 1)].rearrange("t p c n -> (t p) c n")).then_inc(S["l_cv"], 16)
                    e.wait_ge(S["z_ps"], i + 1)
                    e.dma_start(xTs, a["xT"][:, :, bass.ds(i * C, C)]).then_inc(S["l_xt"], 16)
                    e.wait_ge(S["xg"], i + 1)
                    e.dma_start(res, a["xr"][bass.ds(i * C, C), :]).then_inc(S["l_xr"], 16)
                    e.wait_ge(S["x1"], i + 1)
                    e.dma_start(a["d_x1"][bass.ds(i * C, C), :], x1).then_inc(S["x1_st"], 16)
                e.wait_ge(S["qs_ps"], NT + 1)
                e.wait_ge(S["ys_ps"], NT + 1)
                e.wait_ge(S["kkqk_ps"], NT + 1)
                e.dma_start(cv[:, :, 0:TS], a["d_sconv"]).then_inc(S["l_cv"], 16)
                e.wait_ge(S["z_ps"], NT + 1)
                e.dma_start(xTs[:, :, 0:TS], a["xT"][:, :, TP:T]).then_inc(S["l_xt"], 16)
                e.wait_ge(S["xg"], NT + 1)
                e.dma_start(res[0:TS], a["xr"][TP:T, :]).then_inc(S["l_xr"], 16)
                e.wait_ge(S["snew"], NT + 1)
                e.wait_ge(S["hnew"], NT + 1)
                e.dma_start(a["o_pgdn"], St).then_inc(S["p_out"], 16)
                e.dma_start(a["o_pssd"], Ht).then_inc(S["p_out"], 16)
                e.wait_ge(S["z_ps"], NT + 2)
                e.dma_start(Hs, a["state_ssd"]).then_inc(S["sh_in"], 16)
                e.wait_ge(S["x1"], NT + 1)
                e.dma_start(a["d_x1"][TP:T, :], x1[0:TS]).then_inc(S["x1_st"], 16)
                e.wait_ge(S["ss_new"], 4)
                e.wait_ge(S["sh_new"], 4)
                e.dma_start(a["o_sgdn"], Ss[:]).then_inc(S["p_out"], 16)
                e.dma_start(a["o_sssd"], Hs).then_inc(S["p_out"], 16)
                e.wait_ge(S["x1_st"], 16 * NTT + 16)
                e.wait_ge(S["p_out"], 64)
                e.wait_ge(S["z_st"], 16 * NT)

            @block.tensor
            def _(e):
                e.wait_ge(S["m_const"], 16 * (2 * KT + 3))
                e.wait_ge(S["m_zero"], 1)
                with e.Fori(0, NT) as i:
                    n1 = e.snap(i + 1)
                    tile_tensor(e, i, n1, False)
                tile_tensor(e, NT, NT + 1, True)

            @block.scalar
            def _(e):
                with e.Fori(0, NT) as i:
                    n1 = e.snap(i + 1)
                    tile_scalar(e, i, n1, False)
                tile_scalar(e, NT, NT + 1, True)

            @block.vector
            def _(e):
                e.memset(zero, 0.0)
                e.memset(St, 0.0)
                e.memset(Ht, 0.0).then_inc(S["m_zero"], 1)
                e.wait_ge(S["m_const"], 16 * (2 * KT + 3))
                e.wait_ge(S["m_zero"], 1)
                with e.Fori(0, NT) as i:
                    n1 = e.snap(i + 1)
                    tile_vector(e, i, n1, False)
                e.wait_ge(S["gm"], NT + 1)
                e.wait_ge(S["l_cv"], 16 * NTT)
                for g in range(SG):
                    last = e.tensor_tensor(cmk[:, g], bc1(cv[:, 18 + g, 0:TS], P, SB, TS), seqrow[:], ALU.mult)
                last.then_inc(S["ss_cm"], 1)
                tile_vector(e, NT, NT + 1, True)

            @block.gpsimd
            def _(e):
                e.wait_ge(S["m_const"], 16 * (2 * KT + 3))
                with e.Fori(0, NT) as i:
                    n1 = e.snap(i + 1)
                    tile_gpsimd(e, i, n1, False)
                tile_gpsimd(e, NT, NT + 1, True)

        next_stage()
        A = Arena()
        ohp = A(C, 2 * NTT, P)
        ohb = A(C, 2 * NTT, NBMAX)
        iota, tok, valid = A(P, P), A(C, NTT), A(C, NTT)
        before = A(C, C)
        desc = A(C, EPG)
        s3 = [A(C, NTT, EPG) for _ in range(6)]
        g4 = [A(C, NTT, EG) for _ in range(4)]
        col = [A(C, NTT) for _ in range(10)]
        el = A(C, NTT, E)
        oh32 = [A(C, NTT, E) for _ in range(3)]
        tot = [A(P, NTT, E) for _ in range(3)]
        row = [A(P, E) for _ in range(5)]
        cmp_ = A(1, NBMAX, E)
        bexp = A(1, NBMAX)
        dest = A(C, 2, NTT)
        pf = A(C, 2, NTT)
        bf = A(C, 2, NTT)
        rowi = sb("rowi", [P, E], I32)
        pint = sb("pint", [C, 2 * NTT], I32)
        desti = sb("desti", [C, 2 * NTT], I32)
        gates = sb("gates", [C, 2, NTT])
        slot = sb("slot", [P, NBMAX + 1])
        table = sb("table", [1, 2 + NBMAX], I32)
        sem("r_in", "r_v", "r_sub", "r_exp", "r_pe", "r_done")

        def t4(t):
            return t.rearrange("p t (g e) -> p t g e", g=EG)

        begin()
        with nc.Block() as block:
            @block.sync
            def _(e):
                e.dma_start(lnrow[:], a["ln_rows"][:, 2:4, :]).then_inc(S["r_in"], 16)
                for dst, name in ((iota, "c_iota"), (tok, "c_tok"), (valid, "c_valid"), (before, "c_before"), (desc, "c_desc")):
                    e.dma_start(dst, a[name]).then_inc(S["r_in"], 16)

            @block.scalar
            def _(e):
                e.wait_ge(S["r_sub"], 1)
                e.activation(g4[1], g4[1], ACT.Exp).then_inc(S["r_exp"], 1)
                e.wait_ge(S["r_sub"], 2)
                e.activation(col[3], col[3], ACT.Exp).then_inc(S["r_exp"], 1)

            @block.tensor
            def _(e):
                e.wait_ge(S["r_in"], 16 * 6)
                e.wait_ge(S["r_sub"], 3)
                ohs = oh32[2].rearrange("p t e -> p (t e)")
                e.matmul(bank[0][0:C, 0:NTT * E], before, ohs, start=True, stop=True)
                e.matmul(bank[1][:, 0:NTT * E], ones[0:C, :], ohs, start=True, stop=True).then_inc(S["r_pe"], 1)
                e.wait_ge(S["r_sub"], 4)
                for m in range(2 * NTT):
                    last = e.matmul(bank[2][:, 0:NBMAX], ohp[:, m, :], ohb[:, m, :], start=(m == 0), stop=(m == 2 * NTT - 1))
                last.then_inc(S["r_pe"], 1)

            @block.vector
            def _(e):
                done = [0]

                def step(ins):
                    done[0] += 1
                    ins.then_inc(S["r_v"], 1)
                    e.wait_ge(S["r_v"], done[0])

                def first_max(out, x, n, width, m, work):
                    step(e.tensor_reduce(m, x, AX, ALU.max))
                    step(e.tensor_tensor(work, x, bc(m, C, NTT, width), ALU.is_equal))
                    step(e.tensor_tensor(work, work, bc1(desc[:, 0:width], C, NTT, width), ALU.mult))
                    step(e.tensor_reduce(n, work, AX, ALU.max))
                    step(e.tensor_tensor(out, work, bc(n, C, NTT, width), ALU.is_equal))

                e.memset(slot[:], 0.0)
                e.wait_ge(S["r_in"], 16 * 6)
                lg, le = rlog[:, :, 0:EG], rlog[:, :, EG:EG + E]
                first_max(g4[0], lg, col[1], EG, col[0], g4[2])
                step(e.tensor_tensor(g4[1], lg, bc(col[0], C, NTT, EG), ALU.subtract))
                e.tensor_tensor(g4[0], g4[0], bc(valid, C, NTT, EG), ALU.mult).then_inc(S["r_sub"], 1)
                e.wait_ge(S["r_exp"], 1)
                e.wait_ge(S["r_sub"], 1)
                step(e.tensor_reduce(col[2], g4[1], AX, ALU.add))
                step(e.reciprocal(col[2], col[2]))
                step(e.tensor_tensor(t4(el), t4(le), bc(g4[0], C, NTT, EG, EPG), ALU.mult))
                step(e.tensor_reduce(s3[0], t4(el).rearrange("p t g e -> p t e g"), AX, ALU.add))
                first_max(s3[1], s3[0], col[1], EPG, col[4], s3[2])
                step(e.scalar_tensor_tensor(s3[3], s3[1], -3.0e38, s3[0], ALU.mult, ALU.add))
                first_max(s3[4], s3[3], col[1], EPG, col[5], s3[2])
                e.tensor_tensor(col[3], col[5], col[4], ALU.subtract).then_inc(S["r_sub"], 1)
                e.wait_ge(S["r_exp"], 2)
                step(e.tensor_scalar(col[6], col[3], 1.0, None, ALU.add))
                step(e.reciprocal(col[6], col[6]))
                step(e.tensor_tensor(col[6], col[6], col[2], ALU.mult))
                step(e.tensor_scalar(gates[:, 0, :], col[6], 0.5, None, ALU.mult))
                step(e.tensor_tensor(gates[:, 1, :], gates[:, 0, :], col[3], ALU.mult))
                for j, o_ in ((0, s3[1]), (1, s3[4])):
                    step(e.tensor_tensor(t4(oh32[j]), bc(g4[0], C, NTT, EG, EPG), o_.unsqueeze(2).broadcast_to([C, NTT, EG, EPG]), ALU.mult))
                e.tensor_tensor(oh32[2], oh32[0], oh32[1], ALU.add).then_inc(S["r_sub"], 1)
                e.wait_ge(S["r_pe"], 1)
                step(e.tensor_copy(tot[0], bank[1][:, 0:NTT * E].rearrange("p (t e) -> p t e", e=E)))
                step(e.tensor_copy(tot[2], tot[0]))
                src, dst, s_ = 0, 1, 1
                while s_ < NTT:
                    e.tensor_copy(tot[dst][:, 0:s_, :], tot[src][:, 0:s_, :])
                    step(e.tensor_tensor(tot[dst][:, s_:, :], tot[src][:, s_:, :], tot[src][:, 0:NTT - s_, :], ALU.add))
                    src, dst, s_ = dst, src, 2 * s_
                count, nblk, end, first = row[0], row[1], row[2], row[3]
                step(e.tensor_scalar(rowi[:], tot[src][:, NTT - 1, :], float(BLK - 1), None, ALU.add))
                step(e.tensor_scalar(rowi[:], rowi[:], 7, None, ALU.logical_shift_right))
                step(e.tensor_scalar(nblk, rowi[:], 1.0, None, ALU.max))
                step(e.tensor_tensor_scan(end, ones[:, 0:E], nblk, 0.0, ALU.mult, ALU.add))
                step(e.tensor_tensor(first, end, nblk, ALU.subtract))
                step(e.tensor_scalar(first, first, float(BLK), None, ALU.mult))
                step(e.tensor_tensor(tot[dst], tot[src], tot[2], ALU.subtract))
                step(e.tensor_tensor(tot[dst], tot[dst], bc1(first, P, NTT, E), ALU.add))
                step(e.tensor_tensor(tot[dst][0:C], tot[dst][0:C], bank[0][0:C, 0:NTT * E].rearrange("p (t e) -> p t e", e=E), ALU.add))
                for j in range(2):
                    step(e.tensor_tensor(oh32[j], oh32[j], tot[dst][0:C], ALU.mult))
                    step(e.tensor_reduce(dest[:, j, :], oh32[j], AX, ALU.add))
                flat = dest.rearrange("p j t -> p (j t)")
                pff, bff = pf.rearrange("p j t -> p (j t)"), bf.rearrange("p j t -> p (j t)")
                step(e.tensor_copy(desti[:], flat))
                step(e.tensor_scalar(pint[:], desti[:], BLK - 1, None, ALU.bitwise_and))
                step(e.tensor_copy(pff, pint[:]))
                step(e.tensor_scalar(pint[:], desti[:], 7, None, ALU.logical_shift_right))
                step(e.tensor_copy(bff, pint[:]))
                step(e.tensor_tensor(ohp, bc1(iota[0:C], C, 2 * NTT, P), bc(pff, C, 2 * NTT, P), ALU.is_equal))
                step(e.tensor_tensor(ohb, bc1(iota[0:C, 0:NBMAX], C, 2 * NTT, NBMAX), bc(bff, C, 2 * NTT, NBMAX), ALU.is_equal))
                for j in range(2):
                    last = e.tensor_tensor(ohb[:, j * NTT:(j + 1) * NTT], ohb[:, j * NTT:(j + 1) * NTT], bc(tok, C, NTT, NBMAX), ALU.mult)
                last.then_inc(S["r_sub"], 1)
                step(e.tensor_tensor(cmp_, bc1(end[0:1], 1, NBMAX, E), bc(iota[0:1, 0:NBMAX], 1, NBMAX, E), ALU.is_le))
                step(e.tensor_reduce(bexp, cmp_, AX, ALU.add))
                step(e.tensor_scalar(table[0:1, 1:1 + NBMAX], bexp, float(E - 1), None, ALU.min))
                step(e.tensor_scalar(table[0:1, 0:1], end[0:1, E - 1:E], 1.0, None, ALU.subtract))
                e.wait_ge(S["r_pe"], 2)
                step(e.tensor_copy(slot[:, 0:NBMAX], bank[2][:, 0:NBMAX]))

        next_stage()
        A = Arena()
        w1 = A(P, KT, DE)
        w3 = A(P, KT, DE)
        w2 = A(P, DE // P, D)
        xg = A(P, D)
        xgT = A(P, KT, P)
        th = A(P, DE)
        hm = A(P, DE)
        hT = A(P, DE // P, P)
        eo = A(P, D)
        idx = sb("idx", [P, 1], I32)
        sem("w1_in", "w3_in", "w2_in", "e_idx", "e_x", "e_xT_ps", "e_xT", "e_h1", "e_h3", "e_th", "e_s", "e_hm", "e_hT_ps", "e_hT", "e_out", "e_eo", "e_st", "e_go")

        begin()
        with nc.Block() as block:
            def last_block(e):
                return e.value_load(table[0:1, 0:1], min_val=E - 1, max_val=NBMAX - 1)

            @block.sync
            def _(e):
                last = last_block(e)

                def expert(b):
                    return e.value_load(table[0:1, bass.ds(b + 1, 1)], min_val=0, max_val=E - 1)

                def load(dst, src, ex, name):
                    half = dst.shape[1] // 2
                    rows = src.shape[1] // 2
                    for s in range(2):
                        e.dma_start(dst[:, s * half:(s + 1) * half, :],
                                    src[bass.ds(ex, 1), s * rows:(s + 1) * rows, :].rearrange("x (k p) n -> p (x k) n", p=P)).then_inc(S[name], 16)

                ex0, ex1 = expert(0), expert(1)
                load(w1, a["w1"], ex0, "w1_in")
                load(w3, a["w3"], ex0, "w3_in")
                e.wait_ge(S["e_h1"], 1)
                load(w1, a["w1"], ex1, "w1_in")
                e.wait_ge(S["e_h3"], 2)
                load(w3, a["w3"], ex1, "w3_in")
                load(w2, a["w2"], ex0, "w2_in")
                with e.Fori(1, last) as b:
                    b1 = e.snap(b + 1)
                    ex = expert(b1)
                    now = expert(b)
                    e.wait_ge(S["e_h1"], b1)
                    load(w1, a["w1"], ex, "w1_in")
                    e.wait_ge(S["e_h3"], b1 + 1)
                    load(w3, a["w3"], ex, "w3_in")
                    e.wait_ge(S["e_out"], b + 1)
                    load(w2, a["w2"], now, "w2_in")
                ex = expert(last)
                e.wait_ge(S["e_out"], last + 1)
                load(w2, a["w2"], ex, "w2_in")


            @block.gpsimd
            def _(e):
                last = last_block(e)
                with e.Fori(1, last + 3) as n:
                    e.wait_ge(S["e_go"], 1)
                    e.wait_ge(S["e_idx"], n)
                    e.indirect_dma_start(xg, None, a["d_x1"], bass.IndirectOffsetOnAxis(ap=idx[:, 0:1], axis=0)).then_inc(S["e_x"], 16)

            @block.tensor
            def _(e):
                last = last_block(e)

                def x_transpose(b):
                    e.wait_ge(S["e_x"], 16 * (b + 1))
                    e.wait_ge(S["e_xT"], b + 1)
                    for k in range(KT):
                        mm = e.transpose(bank[2 + k // 4][:, (k % 4) * P:(k % 4 + 1) * P], xg[:, k * P:(k + 1) * P], ident[:])
                    mm.then_inc(S["e_xT_ps"], 1)

                def up(b, w, bk, done, arrived):
                    e.wait_ge(S[arrived], 32 * (b + 1))
                    for k in range(KT):
                        mm = e.matmul(bank[bk][:], xgT[:, k, :], w[:, k, :], start=(k == 0), stop=(k == KT - 1))
                    mm.then_inc(S[done], 1)

                def h_transpose(b):
                    e.wait_ge(S["e_hm"], b + 2)
                    e.wait_ge(S["e_hT"], b + 1)
                    for k in range(DE // P):
                        mm = e.transpose(bank[4][:, k * P:(k + 1) * P], hm[:, k * P:(k + 1) * P], ident[:])
                    mm.then_inc(S["e_hT_ps"], 1)

                def down(b):
                    e.wait_ge(S["w2_in"], 32 * (b + 1))
                    e.wait_ge(S["e_hT"], b + 2)
                    e.wait_ge(S["e_eo"], b + 1)
                    for s in range(2):
                        for k in range(DE // P):
                            mm = e.matmul(bank[5 + s][:], hT[:, k, :], w2[:, k, s * 512:(s + 1) * 512], start=(k == 0), stop=(k == DE // P - 1))
                    mm.then_inc(S["e_out"], 1)

                x_transpose(0)
                e.wait_ge(S["e_xT"], 2)
                up(0, w1, 0, "e_h1", "w1_in")
                up(0, w3, 1, "e_h3", "w3_in")
                x_transpose(1)
                with e.Fori(1, last + 1) as b:
                    b1 = e.snap(b + 1)
                    e.wait_ge(S["e_xT"], b1 + 1)
                    e.wait_ge(S["e_hm"], b + 1)
                    up(b, w1, 0, "e_h1", "w1_in")
                    h_transpose(b - 1)
                    up(b, w3, 1, "e_h3", "w3_in")
                    x_transpose(b1)
                    down(b - 1)
                h_transpose(last)
                down(last)
                e.wait_ge(S["e_st"], 16 * (last + 1) + 16)

            @block.scalar
            def _(e):
                last = last_block(e)

                def x_copy(b):
                    e.wait_ge(S["e_xT_ps"], b + 2)
                    e.wait_ge(S["e_h3"], b + 1)
                    for s in range(2):
                        copy = e.activation(xgT[:, 4 * s:4 * s + 4, :].rearrange("p k n -> p (k n)"), bank[2 + s][:], ACT.Copy)
                    copy.then_inc(S["e_xT"], 1)

                def tanh(b):
                    e.wait_ge(S["e_h1"], b + 1)
                    e.wait_ge(S["e_s"], b + 1)
                    e.activation(th, bank[0][:], ACT.Tanh, scale=0.5).then_inc(S["e_th"], 1)

                def h_copy(b):
                    e.wait_ge(S["e_hT_ps"], b + 2)
                    e.wait_ge(S["e_out"], b + 1)
                    e.activation(hT.rearrange("p k n -> p (k n)"), bank[4][:], ACT.Copy).then_inc(S["e_hT"], 1)

                def out_copy(b):
                    e.wait_ge(S["e_out"], b + 2)
                    e.wait_ge(S["e_st"], 16 * b + 16)
                    for s in range(2):
                        copy = e.activation(eo[:, s * 512:(s + 1) * 512], bank[5 + s][:], ACT.Copy)
                    copy.then_inc(S["e_eo"], 1)
                    e.wait_ge(S["e_eo"], b + 2)
                    e.dma_start(a["d_eo"][bass.ds(b * BLK, BLK), :], eo).then_inc(S["e_st"], 16)

                x_copy(0)
                tanh(0)
                x_copy(1)
                with e.Fori(1, last + 1) as b:
                    b1 = e.snap(b + 1)
                    bm = e.snap(b - 1)
                    tanh(b)
                    h_copy(bm)
                    x_copy(b1)
                    out_copy(bm)
                h_copy(last)
                out_copy(last)

            @block.vector
            def _(e):
                last = last_block(e)

                def take(b):
                    e.wait_ge(S["e_x"], 16 * b)
                    e.wait_ge(S["e_xT_ps"], b + 1)
                    e.tensor_scalar(idx[:], slot[:, bass.ds(b, 1)], 1.0, None, ALU.mult).then_inc(S["e_idx"], 1)

                def gate(b):
                    e.wait_ge(S["e_th"], b + 1)
                    e.wait_ge(S["e_hT_ps"], b + 1)
                    e.scalar_tensor_tensor(hm, th, 1.0, bank[0][:], ALU.add, ALU.mult).then_inc(S["e_s"], 1)
                    e.wait_ge(S["e_s"], b + 2)
                    e.wait_ge(S["e_h3"], b + 2)
                    e.tensor_tensor(hm, hm, bank[1][:], ALU.mult).then_inc(S["e_hm"], 1)

                e.memset(th[0:1, 0:1], 0.0).then_inc(S["e_go"], 1)
                take(0)
                take(1)
                gate(0)
                with e.Fori(1, last + 1) as b:
                    take(b + 1)
                    gate(b)

        next_stage()
        A = Arena()
        r0 = [A(C, D) for _ in range(2)]
        r1 = [A(C, D) for _ in range(2)]
        xa = [A(C, D) for _ in range(2)]
        yo = [A(C, D) for _ in range(2)]
        gcol = [A(C, 2) for _ in range(2)]
        st = [A(C, 2, 6) for _ in range(2)]
        mv2 = [A(C, 2) for _ in range(2)]
        rv = [A(C, 4) for _ in range(2)]
        cidx = [sb(f"cidx{r}", [C, 2], I32) for r in range(2)]
        names = ("c_idx", "c_r", "c_x", "c_xa", "c_t", "c_sum", "c_st", "c_mv", "c_mve", "c_rstd", "c_nmr", "c_xn", "c_g", "c_y", "c_out")
        for r in range(2):
            sem(*[f"{n}{r}" for n in names])
        sem("c_go")

        begin()
        with nc.Block() as block:
            def step_vector(e, r, j, j1, t, n):
                e.wait_ge(S[f"c_sum{r}"], j + 1)
                if n == C:
                    for q in range(2):
                        e.tensor_scalar(gcol[r][:, q:q + 1], gates[:, q, bass.ds(t, 1)], 1.0, None, ALU.mult)
                        last = e.tensor_scalar(cidx[r][:, q:q + 1], desti[:, bass.ds(t + q * NTT, 1)], 1.0, None, ALU.mult)
                else:
                    for q in range(2):
                        e.tensor_scalar(gcol[r][0:n, q:q + 1], gates[0:n, q, t:t + 1], 1.0, None, ALU.mult)
                        last = e.tensor_scalar(cidx[r][0:n, q:q + 1], desti[0:n, t + q * NTT:t + q * NTT + 1], 1.0, None, ALU.mult)
                last.then_inc(S[f"c_idx{r}"], 1)

            def sums(e, r, j, j1, n):
                e.wait_ge(S[f"c_r{r}"], 32 * j1)
                e.wait_ge(S[f"c_xa{r}"], j1)
                e.wait_ge(S[f"c_idx{r}"], j1)
                e.scalar_tensor_tensor(xa[r][0:n], r0[r][0:n], gcol[r][0:n, 0:1], xa[r][0:n], ALU.mult, ALU.add).then_inc(S[f"c_t{r}"], 1)
                e.wait_ge(S[f"c_t{r}"], j1)
                e.scalar_tensor_tensor(xa[r][0:n], r1[r][0:n], gcol[r][0:n, 1:2], xa[r][0:n], ALU.mult, ALU.add).then_inc(S[f"c_sum{r}"], 1)
                e.wait_ge(S[f"c_sum{r}"], j1 + 1)
                for s in range(2):
                    last = e.bn_stats(st[r][0:n, s, :], xa[r][0:n, s * 512:(s + 1) * 512])
                last.then_inc(S[f"c_st{r}"], 1)
                e.wait_ge(S["c_go"], 1)
                e.wait_ge(S[f"c_st{r}"], j1)
                e.bn_aggr(mv2[r][0:n], st[r][0:n].rearrange("p a b -> p (a b)")).then_inc(S[f"c_mv{r}"], 1)
                e.wait_ge(S[f"c_mv{r}"], j1)
                e.tensor_scalar(rv[r][0:n, 0:1], mv2[r][0:n, 1:2], EPS, None, ALU.add).then_inc(S[f"c_mve{r}"], 1)
                e.wait_ge(S[f"c_rstd{r}"], j1)
                e.scalar_tensor_tensor(rv[r][0:n, 2:3], mv2[r][0:n, 0:1], -1.0, rv[r][0:n, 1:2], ALU.mult, ALU.mult).then_inc(S[f"c_nmr{r}"], 1)
                e.wait_ge(S[f"c_g{r}"], j1 + 1)
                e.tensor_tensor(yo[r][0:n], yo[r][0:n], lnrow[0:n, 1, :], ALU.add).then_inc(S[f"c_y{r}"], 1)

            def gathers(e, r, j1, n):
                e.wait_ge(S["c_go"], 1)
                e.wait_ge(S[f"c_idx{r}"], j1)
                e.indirect_dma_start(r0[r][0:n], None, a["d_eo"], bass.IndirectOffsetOnAxis(ap=cidx[r][0:n, 0:1], axis=0)).then_inc(S[f"c_r{r}"], 16)
                e.indirect_dma_start(r1[r][0:n], None, a["d_eo"], bass.IndirectOffsetOnAxis(ap=cidx[r][0:n, 1:2], axis=0)).then_inc(S[f"c_r{r}"], 16)

            def scale(e, r, j, j1, n):
                e.wait_ge(S[f"c_mve{r}"], j1)
                e.tensor_tensor(rv[r][0:n, 1:2], rv[r][0:n, 0:1], mhalf[0:n, 0:1], ALU.pow).then_inc(S[f"c_rstd{r}"], 1)
                e.wait_ge(S[f"c_xn{r}"], j1)
                e.wait_ge(S[f"c_out{r}"], 16 * j + 16)
                e.tensor_tensor(yo[r][0:n], xa[r][0:n], lnrow[0:n, 0, :], ALU.mult).then_inc(S[f"c_g{r}"], 1)

            def acts(e, r, j, j1, n, half):
                if half == 0:
                    e.wait_ge(S[f"c_x{r}"], 16 * j1)
                    e.activation(xa[r][0:n], xa[r][0:n], ACT.Copy, scale=ALPHA).then_inc(S[f"c_xa{r}"], 1)
                else:
                    e.wait_ge(S[f"c_nmr{r}"], j1)
                    e.activation(xa[r][0:n], xa[r][0:n], ACT.Identity, bias=rv[r][0:n, 2:3], scale=rv[r][0:n, 1:2]).then_inc(S[f"c_xn{r}"], 1)

            ROUNDS = NT // 2

            @block.sync
            def _(e):
                with e.Fori(0, ROUNDS) as j:
                    j1 = e.snap(j + 1)
                    for r in range(2):
                        e.wait_ge(S[f"c_g{r}"], j + 1)
                        e.dma_start(xa[r], a["d_x1"][bass.ds((2 * j + r) * C, C), :]).then_inc(S[f"c_x{r}"], 16)
                    for r in range(2):
                        e.wait_ge(S[f"c_y{r}"], j1)
                        e.dma_start(a["o_y"][bass.ds((2 * j + r) * C, C), :], yo[r]).then_inc(S[f"c_out{r}"], 16)
                e.wait_ge(S["c_g0"], ROUNDS + 1)
                e.dma_start(xa[0][0:TS], a["d_x1"][TP:T, :]).then_inc(S["c_x0"], 16)
                e.wait_ge(S["c_y0"], ROUNDS + 1)
                e.dma_start(a["o_y"][TP:T, :], yo[0][0:TS]).then_inc(S["c_out0"], 16)
                e.wait_ge(S["c_out0"], 16 * (ROUNDS + 1) + 16)
                e.wait_ge(S["c_out1"], 16 * ROUNDS + 16)

            @block.gpsimd
            def _(e):
                with e.Fori(1, ROUNDS + 1) as j1:
                    for r in range(2):
                        gathers(e, r, j1, C)
                    j = e.snap(j1 - 1)
                    for r in range(2):
                        scale(e, r, j, j1, C)
                gathers(e, 0, ROUNDS + 1, TS)
                scale(e, 0, ROUNDS, ROUNDS + 1, TS)

            @block.scalar
            def _(e):
                with e.Fori(0, ROUNDS) as j:
                    j1 = e.snap(j + 1)
                    for half in range(2):
                        for r in range(2):
                            acts(e, r, j, j1, C, half)
                for half in range(2):
                    acts(e, 0, ROUNDS, ROUNDS + 1, TS, half)

            @block.vector
            def _(e):
                e.memset(rv[0][0:1, 3:4], 0.0).then_inc(S["c_go"], 1)
                with e.Fori(0, ROUNDS) as j:
                    j1 = e.snap(j + 1)
                    for r in range(2):
                        step_vector(e, r, j, j1, 2 * j + r, C)
                    for r in range(2):
                        sums(e, r, j, j1, C)
                step_vector(e, 0, ROUNDS, ROUNDS + 1, NT, TS)
                sums(e, 0, ROUNDS, ROUNDS + 1, TS)


OUTPUTS = {
    "o_y": (T, D), "o_pgdn": (P, GH, DK), "o_pssd": (P, SH * SP_), "o_pconv": (P, CT, CW - 1),
    "o_sgdn": (P, SB, GH, DK), "o_sssd": (P, SB, SH * SP_), "o_sconv": (P, CT, SB, CW - 1)}
SCRATCH = {"d_conv": (NT, P, CT, C), "d_sconv": (P, CT, TS), "d_x1": (T, D), "d_eo": ((E + 2 * NT) * BLK, D)}


def layouts(i):
    f = {k: np.asarray(v) for k, v in i.items()}
    x = np.concatenate([f["meta_tokens"], f["x_prompt"][0], f["x_sample"].reshape(TS, D)], 0)
    w = f["w_in"][0]
    qkv, z_a, b_a, a_a, z_b, xbc, dt_b = np.split(w, np.cumsum([1536, 512, GH, GH, 512, 1024]), axis=1)

    def kp(m):
        return m.reshape(-1, P, m.shape[1]).transpose(1, 0, 2)

    def rows(*v):
        return np.broadcast_to(np.stack(v, 0)[None], (P, len(v), v[0].shape[0]))

    wc = np.concatenate([qkv, xbc], 1)
    cw = np.concatenate([f["gdn_conv_w"][0], f["ssd_conv_w"][0]], 1)
    cb = np.concatenate([np.zeros(1536, np.float32), f["ssd_conv_b"][0]])
    past = np.concatenate([f["state_gdn_conv"][0], f["state_ssd_conv"][0]], 2)
    out = {
        "xT": kp(x.T), "xr": x,
        "w_conv": wc.reshape(KT, P, CT, P).transpose(2, 1, 0, 3),
        "w_z": kp(np.concatenate([z_a, z_b], 1)),
        "w_small": kp(np.concatenate([b_a, a_a, dt_b], 1)),
        "conv_w": cw.reshape(CW, CT, P).transpose(2, 1, 0),
        "conv_b": cb.reshape(CT, P).T,
        "conv_past": past.reshape(SB, CW - 1, CT, P).transpose(3, 2, 0, 1),
        "head_bias": rows(np.concatenate([f["gdn_dt_bias"][0], f["ssd_dt_bias"][0]]))[:, 0],
        "head_alog": rows(np.concatenate([f["gdn_a_log"][0], f["ssd_a_log"][0]]))[:, 0],
        "head_rows": rows(np.tile(f["gdn_norm_w"][0], GH), f["ssd_norm_w"][0]),
        "ssd_d": rows(f["ssd_d"][0])[:, 0],
        "ln_rows": rows(f["ln1_g"][0], f["ln1_b"][0], f["ln2_g"][0], f["ln2_b"][0]),
        "w_out": kp(f["w_out"][0]),
        "w_router": kp(np.concatenate([f["router_g"][0], f["router_e"][0]], 1)),
        "w1": f["w1"][0], "w3": f["w3"][0], "w2": f["w2"][0],
        "state_gdn": f["state_gdn"][0].transpose(2, 0, 1, 3),
        "state_ssd": f["state_ssd"][0].transpose(3, 0, 1, 2).reshape(SN, SB, SH * SP_),
    }
    out.update(constants())
    return {k: np.ascontiguousarray(v) for k, v in out.items()}


def kernel(**inputs):
    import concourse.bacc as bacc
    from concourse.bass_utils import run_bass_kernel_spmd

    nc = bacc.Bacc("TRN2", target_bir_lowering=False, num_devices=1)
    arrays = layouts(inputs)
    aps = {n: nc.dram_tensor(n, v.shape, mybir.dt.from_np(v.dtype), kind="ExternalInput").ap() for n, v in arrays.items()}
    aps.update({n: nc.dram_tensor(n, s, F32, kind="ExternalOutput").ap() for n, s in OUTPUTS.items()})
    aps.update({n: nc.dram_tensor(n, s, F32, kind="Internal").ap() for n, s in SCRATCH.items()})
    program(nc, aps)
    got = run_bass_kernel_spmd(nc, [arrays], core_ids=[0]).results[0]
    y = got["o_y"]
    pconv = got["o_pconv"].transpose(2, 1, 0).reshape(1, 1, CW - 1, CT * P)
    sconv = got["o_sconv"].transpose(2, 3, 1, 0).reshape(1, SB, CW - 1, CT * P)
    return (
        y[META:TP].reshape(1, SEQ, D), y[TP:T].reshape(SB, SL, D),
        got["o_pgdn"].transpose(1, 0, 2).reshape(1, 1, GH, DK, DK), pconv[..., :1536],
        got["o_pssd"].reshape(SN, SH, SP_).transpose(1, 2, 0).reshape(1, 1, SH, SP_, SN), pconv[..., 1536:],
        got["o_sgdn"].transpose(1, 2, 0, 3).reshape(1, SB, GH, DK, DK), sconv[..., :1536],
        got["o_sssd"].reshape(SN, SB, SH, SP_).transpose(1, 2, 3, 0).reshape(1, SB, SH, SP_, SN), sconv[..., 1536:])
```
